# Optimizing a Trainium2 kernel written in Bass

```python
import jax, jax.numpy as jnp
from jax import lax
import numpy as np

D_MODEL = 1024
BATCH = 1
SEQ = 512
DEPTH = 1

HEAD_DIM = 64
ATT_SLOTS = 8
DIL_PATTERNS = ((128, 1), (512, 4), (2048, 16))
N_DIL = 3
ATT_SUBHEADS = ATT_SLOTS * N_DIL
ATT_BLOCK = 128
ATT_Q = ATT_SUBHEADS * HEAD_DIM
ATT_KV = ATT_SLOTS * HEAD_DIM
ALIBI_MAX_EXP = 8.0
CONV_CH = 512
CONV_K = 31
MLSTM_HEADS = 4
MLSTM_DH = 128
MLSTM_W = MLSTM_HEADS * MLSTM_DH
MLSTM_CONV_K = 4
MLSTM_CHUNK = 128
N_BRANCH = 3
N_GROUPS_MOE = 4
EXPERTS_PER_GROUP = 8
N_EXPERTS = N_GROUPS_MOE * EXPERTS_PER_GROUP
TOP_K = 2
D_EXPERT = 256
MOE_BLOCK = 128
PLE_DIM = 256
EPS = 1e-6

SPLITS = (ATT_Q, ATT_KV, ATT_KV, 2 * CONV_CH, MLSTM_W, MLSTM_W, MLSTM_W, MLSTM_W,
          MLSTM_HEADS, MLSTM_HEADS, N_BRANCH * D_MODEL)
D_IN = sum(SPLITS)
SPLIT_IDX = tuple(int(c) for c in np.cumsum(SPLITS)[:-1])

kernel_name = "hybrid_dilated_conv_mlstm_hmoe"

def rmsnorm(x, g):
    xf = x.astype(jnp.float32)
    r = lax.rsqrt(jnp.mean(xf * xf, axis=-1, keepdims=True) + EPS)
    return (xf * r).astype(x.dtype) * g

def layernorm(x, g, b):
    xf = x.astype(jnp.float32)
    mu = jnp.mean(xf, axis=-1, keepdims=True)
    var = jnp.mean(jnp.square(xf - mu), axis=-1, keepdims=True)
    return ((xf - mu) * lax.rsqrt(var + EPS)).astype(x.dtype) * g + b

def causal_dwconv(x, w, b):
    k, c = w.shape
    y = lax.conv_general_dilated(x, w[:, None, :], window_strides=(1,), padding=((k - 1, 0),),
                                 dimension_numbers=("NWC", "WIO", "NWC"), feature_group_count=c)
    return y + b

def alibi_slopes():
    j = jnp.arange(1, ATT_SUBHEADS + 1, dtype=jnp.float32)
    return (2.0 ** (-ALIBI_MAX_EXP * j / ATT_SUBHEADS)).reshape(N_DIL, ATT_SLOTS)

def _window_attend(q, k, v, slopes, dilation, steps):
    n, l, h, hd = q.shape
    nb = l // ATT_BLOCK
    qb = q.reshape(n, nb, ATT_BLOCK, h, hd)
    kb = k.reshape(n, nb, ATT_BLOCK, h, hd)
    vb = v.reshape(n, nb, ATT_BLOCK, h, hd)
    prev = ((0, 0), (1, 0), (0, 0), (0, 0), (0, 0))
    k2 = jnp.concatenate([jnp.pad(kb[:, :-1], prev), kb], axis=2)
    v2 = jnp.concatenate([jnp.pad(vb[:, :-1], prev), vb], axis=2)
    qi = jnp.arange(ATT_BLOCK)[:, None] + ATT_BLOCK
    ki = jnp.arange(2 * ATT_BLOCK)[None, :]
    dist = qi - ki
    kabs = jnp.arange(nb)[:, None, None] * ATT_BLOCK + ki[None] - ATT_BLOCK
    valid = (dist >= 0) & (dist <= steps) & (kabs >= 0)
    bias = -(slopes[:, None, None] * (dilation * dist).astype(jnp.float32))
    s = jnp.einsum("nbqhd,nbkhd->nbhqk", qb, k2).astype(jnp.float32) + bias
    s = jnp.where(valid[None, :, None], s, -jnp.inf)
    m = jnp.max(s, axis=-1, keepdims=True)
    pr = jnp.exp(s - m)
    den = jnp.sum(pr, axis=-1, keepdims=True)
    o = jnp.einsum("nbhqk,nbkhd->nbqhd", pr / den, v2.astype(jnp.float32))
    lse = (m + jnp.log(den))[..., 0]
    return o.reshape(n, l, h, hd), lse.transpose(0, 1, 3, 2).reshape(n, l, h)

def dilated_attention(q, k, v):
    b, s = q.shape[0], q.shape[1]
    slopes = alibi_slopes()
    q = q * HEAD_DIM ** -0.5
    outs, lses = [], []
    for g, (window, dil) in enumerate(DIL_PATTERNS):
        l = s // dil
        lp = -(-l // ATT_BLOCK) * ATT_BLOCK

        def to_sub(t):
            t = t.reshape(b, l, dil, ATT_SLOTS, HEAD_DIM).transpose(0, 2, 1, 3, 4)
            t = t.reshape(b * dil, l, ATT_SLOTS, HEAD_DIM)
            return jnp.pad(t, ((0, 0), (0, lp - l), (0, 0), (0, 0)))

        o, lse = _window_attend(to_sub(q[:, :, g]), to_sub(k), to_sub(v), slopes[g], dil, window // dil)
        o = o[:, :l].reshape(b, dil, l, ATT_SLOTS, HEAD_DIM).transpose(0, 2, 1, 3, 4)
        lse = lse[:, :l].reshape(b, dil, l, ATT_SLOTS).transpose(0, 2, 1, 3)
        outs.append(o.reshape(b, s, ATT_SLOTS, HEAD_DIM))
        lses.append(lse.reshape(b, s, ATT_SLOTS))
    wts = jax.nn.softmax(jnp.stack(lses, axis=0), axis=0)
    o = jnp.einsum("gbsh,gbshd->bshd", wts, jnp.stack(outs, axis=0))
    return o.reshape(b, s, ATT_SLOTS * HEAD_DIM).astype(k.dtype)

def conformer_conv(u, dw_w, dw_b, ln_g, ln_b):
    a, gt = jnp.split(u, 2, axis=-1)
    y = a * jax.nn.sigmoid(gt)
    y = causal_dwconv(y, dw_w, dw_b)
    y = layernorm(y, ln_g, ln_b)
    return jax.nn.silu(y)

def mlstm(q, k, v, i_pre, f_pre):
    b, s, h, dh = q.shape
    lc = MLSTM_CHUNK
    nc = s // lc
    f32 = jnp.float32

    def chunks(t):
        return t.astype(f32).reshape(b, nc, lc, h, -1).transpose(0, 3, 1, 2, 4)

    def gchunks(t):
        return t.astype(f32).reshape(b, nc, lc, h).transpose(0, 3, 1, 2)

    qc, kc, vc = chunks(q), chunks(k) * dh ** -0.5, chunks(v)
    ig = gchunks(i_pre)
    lf = jax.nn.log_sigmoid(gchunks(f_pre))
    bcum = jnp.cumsum(lf, axis=-1)
    gtot = bcum[..., -1]
    causal = jnp.tril(jnp.ones((lc, lc), dtype=bool))
    dmat = bcum[..., :, None] - bcum[..., None, :] + ig[..., None, :]
    dmat = jnp.where(causal, dmat, -jnp.inf)
    wst = gtot[..., None] - bcum + ig
    m_loc = jnp.max(wst, axis=-1)
    e = jnp.exp(wst - m_loc[..., None])
    c_loc = jnp.einsum("bhcl,bhclv,bhclk->bhcvk", e, vc, kc)
    n_loc = jnp.einsum("bhcl,bhclk->bhck", e, kc)

    def step(carry, inp):
        c_prev, n_prev, m_prev = carry
        cl, nl, ml, gc = inp
        m_new = jnp.maximum(gc + m_prev, ml)
        a = jnp.exp(gc + m_prev - m_new)
        bb = jnp.exp(ml - m_new)
        c_new = a[..., None, None] * c_prev + bb[..., None, None] * cl
        n_new = a[..., None] * n_prev + bb[..., None] * nl
        return (c_new, n_new, m_new), (c_prev, n_prev, m_prev)

    init = (jnp.zeros((b, h, dh, dh), f32), jnp.zeros((b, h, dh), f32), jnp.zeros((b, h), f32))
    xs = (jnp.moveaxis(c_loc, 2, 0), jnp.moveaxis(n_loc, 2, 0), jnp.moveaxis(m_loc, 2, 0), jnp.moveaxis(gtot, 2, 0))
    _, (c_st, n_st, m_st) = lax.scan(step, init, xs)
    c_st = jnp.moveaxis(c_st, 0, 2)
    n_st = jnp.moveaxis(n_st, 0, 2)
    m_st = jnp.moveaxis(m_st, 0, 2)
    a_inter = bcum + m_st[..., None]
    m_t = jnp.maximum(a_inter, jnp.max(dmat, axis=-1))
    w_intra = jnp.exp(dmat - m_t[..., None])
    sc = jnp.einsum("bhcqd,bhckd->bhcqk", qc, kc) * w_intra
    s_inter = jnp.exp(a_inter - m_t)
    num = jnp.einsum("bhcqk,bhckv->bhcqv", sc, vc) + s_inter[..., None] * jnp.einsum("bhcvk,bhcqk->bhcqv", c_st, qc)
    den = jnp.sum(sc, axis=-1) + s_inter * jnp.einsum("bhck,bhcqk->bhcq", n_st, qc)
    hout = num / jnp.maximum(jnp.abs(den), jnp.exp(-m_t))[..., None]
    return hout.transpose(0, 2, 3, 1, 4).reshape(b, s, h * dh).astype(q.dtype)

def expert_dispatch(xf, eid, wts, w_gate, w_up, w_down):
    t, d = xf.shape
    a = t * TOP_K
    e_flat = eid.reshape(a)
    tok = jnp.arange(a, dtype=jnp.int32) // TOP_K
    order = jnp.argsort(e_flat)
    e_sorted = e_flat[order]
    counts = jnp.zeros((N_EXPERTS,), jnp.int32).at[e_flat].add(1)
    padded = (counts + MOE_BLOCK - 1) // MOE_BLOCK * MOE_BLOCK
    start = jnp.cumsum(counts) - counts
    ends_p = jnp.cumsum(padded)
    pstart = ends_p - padded
    dest = pstart[e_sorted] + (jnp.arange(a, dtype=jnp.int32) - start[e_sorted])
    p_len = a + N_EXPERTS * MOE_BLOCK
    nb = p_len // MOE_BLOCK
    buf_tok = jnp.full((p_len,), t, jnp.int32).at[dest].set(tok[order])
    buf_w = jnp.zeros((p_len,), xf.dtype).at[dest].set(wts.reshape(a)[order].astype(xf.dtype))
    blk_e = jnp.minimum(jnp.searchsorted(ends_p, jnp.arange(nb, dtype=jnp.int32) * MOE_BLOCK, side="right"), N_EXPERTS - 1)
    x_pad = jnp.concatenate([xf, jnp.zeros((1, d), xf.dtype)], axis=0)

    def run_block(args):
        idx, e, w = args
        xb = x_pad[idx]
        hb = jax.nn.silu(xb @ w_gate[e]) * (xb @ w_up[e])
        return (hb @ w_down[e]) * w[:, None]

    yb = lax.map(run_block, (buf_tok.reshape(nb, MOE_BLOCK), blk_e, buf_w.reshape(nb, MOE_BLOCK)))
    out = jnp.zeros((t + 1, d), yb.dtype).at[buf_tok].add(yb.reshape(p_len, d))
    return out[:t]

def hier_moe(h, w_rg, b_rg, w_re, b_re, w_gate, w_up, w_down):
    b, s, d = h.shape
    t = b * s
    hf = h.reshape(t, d)
    rows = jnp.arange(t)
    lg = (hf @ w_rg).astype(jnp.float32) + b_rg
    pg = jax.nn.softmax(lg, axis=-1)
    _, g_sel = lax.top_k(lg, 1)
    g_sel = g_sel[:, 0]
    p_g = pg[rows, g_sel]
    le = ((hf @ w_re).astype(jnp.float32) + b_re).reshape(t, N_GROUPS_MOE, EXPERTS_PER_GROUP)
    le_sel = le[rows, g_sel]
    top_v, top_i = lax.top_k(le_sel, TOP_K)
    wts = p_g[:, None] * jax.nn.softmax(top_v, axis=-1)
    eid = g_sel[:, None] * EXPERTS_PER_GROUP + top_i
    return expert_dispatch(hf, eid, wts, w_gate, w_up, w_down).reshape(b, s, d)

def setup_inputs(seed: int = 0) -> dict:
    key = jax.random.key(seed)
    ks = jax.random.split(key, 28)
    f32 = jnp.float32
    L, D = DEPTH, D_MODEL

    def nrm(k, shape, scale):
        return jax.random.normal(k, shape, f32) * scale

    def gain(k, shape):
        return 1.0 + 0.05 * jax.random.normal(k, shape, f32)

    return {
        "x": nrm(ks[0], (BATCH, SEQ, D), 1.0),
        "p": nrm(ks[1], (DEPTH, BATCH, SEQ, PLE_DIM), 1.0),
        "g_mix": gain(ks[2], (L, D)),
        "w_in": nrm(ks[3], (L, D, D_IN), D ** -0.5),
        "conv_w": nrm(ks[4], (L, CONV_K, CONV_CH), CONV_K ** -0.5),
        "conv_b": nrm(ks[5], (L, CONV_CH), 0.02),
        "conv_ln_g": gain(ks[6], (L, CONV_CH)),
        "conv_ln_b": nrm(ks[7], (L, CONV_CH), 0.02),
        "mlstm_conv_w": nrm(ks[8], (L, MLSTM_CONV_K, 2 * MLSTM_W), MLSTM_CONV_K ** -0.5),
        "mlstm_conv_b": nrm(ks[9], (L, 2 * MLSTM_W), 0.02),
        "mlstm_i_bias": nrm(ks[10], (L, MLSTM_HEADS), 0.1),
        "mlstm_f_bias": jnp.linspace(3.0, 6.0, MLSTM_HEADS, dtype=f32) + nrm(ks[11], (L, MLSTM_HEADS), 0.1),
        "w_br_att": nrm(ks[12], (L, ATT_KV, D), ATT_KV ** -0.5),
        "w_br_conv": nrm(ks[13], (L, CONV_CH, D), CONV_CH ** -0.5),
        "w_br_mlstm": nrm(ks[14], (L, MLSTM_W, D), MLSTM_W ** -0.5),
        "w_out": nrm(ks[15], (L, D, D), D ** -0.5),
        "g_ffn": gain(ks[16], (L, D)),
        "w_router_g": nrm(ks[17], (L, D, N_GROUPS_MOE), D ** -0.5),
        "b_router_g": nrm(ks[18], (L, N_GROUPS_MOE), 0.01),
        "w_router_e": nrm(ks[19], (L, D, N_EXPERTS), D ** -0.5),
        "b_router_e": nrm(ks[20], (L, N_EXPERTS), 0.01),
        "w_exp_gate": nrm(ks[21], (L, N_EXPERTS, D, D_EXPERT), D ** -0.5),
        "w_exp_up": nrm(ks[22], (L, N_EXPERTS, D, D_EXPERT), D ** -0.5),
        "w_exp_down": nrm(ks[23], (L, N_EXPERTS, D_EXPERT, D), D_EXPERT ** -0.5),
        "g_ple": gain(ks[24], (L, D)),
        "w_ple_gate": nrm(ks[25], (L, D, D), D ** -0.5),
        "w_ple_proj": nrm(ks[26], (L, PLE_DIM, D), PLE_DIM ** -0.5),
        "g_final": gain(ks[27], (D,)),
    }

def reference(x, p, g_mix, w_in, conv_w, conv_b, conv_ln_g, conv_ln_b, mlstm_conv_w, mlstm_conv_b,
              mlstm_i_bias, mlstm_f_bias, w_br_att, w_br_conv, w_br_mlstm, w_out, g_ffn,
              w_router_g, b_router_g, w_router_e, b_router_e, w_exp_gate, w_exp_up, w_exp_down,
              g_ple, w_ple_gate, w_ple_proj, g_final):
    b, s, d = x.shape
    for i in range(DEPTH):
        h = rmsnorm(x, g_mix[i])
        proj = h @ w_in[i]
        (q_a, k_a, v_a, u_conv, q_m, k_m, v_m, o_m, i_m, f_m, gate_pre) = jnp.split(proj, SPLIT_IDX, axis=-1)
        y_att = dilated_attention(q_a.reshape(b, s, N_DIL, ATT_SLOTS, HEAD_DIM),
                                  k_a.reshape(b, s, ATT_SLOTS, HEAD_DIM),
                                  v_a.reshape(b, s, ATT_SLOTS, HEAD_DIM))
        y_conv = conformer_conv(u_conv, conv_w[i], conv_b[i], conv_ln_g[i], conv_ln_b[i])
        qk = jax.nn.silu(causal_dwconv(jnp.concatenate([q_m, k_m], axis=-1), mlstm_conv_w[i], mlstm_conv_b[i]))
        q_c, k_c = jnp.split(qk, 2, axis=-1)
        h_m = mlstm(q_c.reshape(b, s, MLSTM_HEADS, MLSTM_DH), k_c.reshape(b, s, MLSTM_HEADS, MLSTM_DH),
                    v_m.reshape(b, s, MLSTM_HEADS, MLSTM_DH), i_m + mlstm_i_bias[i], f_m + mlstm_f_bias[i])
        y_m = jax.nn.sigmoid(o_m) * h_m
        gates = jax.nn.sigmoid(gate_pre).reshape(b, s, N_BRANCH, d)
        merged = (gates[..., 0, :] * (y_att @ w_br_att[i])
                  + gates[..., 1, :] * (y_conv @ w_br_conv[i])
                  + gates[..., 2, :] * (y_m @ w_br_mlstm[i]))
        x = x + merged @ w_out[i]
        h2 = rmsnorm(x, g_ffn[i])
        x = x + hier_moe(h2, w_router_g[i], b_router_g[i], w_router_e[i], b_router_e[i],
                         w_exp_gate[i], w_exp_up[i], w_exp_down[i])
        hp = rmsnorm(x, g_ple[i])
        x = x + jax.nn.sigmoid(hp @ w_ple_gate[i]) * (p[i] @ w_ple_proj[i])
    return rmsnorm(x, g_final)


_drawn_inputs = setup_inputs


def setup_inputs(seed=0):
    import zlib

    import numpy as np

    out = dict(_drawn_inputs(seed))
    spreads = {}
    factors = {'conv_ln_b': 3.09,
     'mlstm_conv_b': 17.046,
     'mlstm_i_bias': 48.616,
     'b_router_g': 3.123,
     'b_router_e': 3.452,
     'g_ple': 6.64}
    for name, (base, spread) in spreads.items():
        noise = np.random.default_rng([zlib.crc32(name.encode()), seed]).standard_normal(out[name].shape)
        drawn = base * np.exp(spread * noise) if base else spread * noise
        out[name] = __import__('jax').numpy.asarray(drawn.astype(out[name].dtype))
    for name, factor in factors.items():
        out[name] = (out[name] * factor).astype(out[name].dtype)
    return out
```

```python
from contextlib import ExitStack

import numpy as np

import concourse.bass as bass
from concourse import mybir

F32 = mybir.dt.float32
I32 = mybir.dt.int32
ALU = mybir.AluOpType
ACT = mybir.ActivationFunctionType
AXX = mybir.AxisListType.X

P = 128
D = 1024
SEQ = 512
T = SEQ // P
KD = D // P
HEAD = 64
SLOTS = 8
DILATIONS = (1, 4, 16)
STEPS = 128
ROUNDS = 4
CH = 512
CONV_K = 31
MCONV_K = 4
DH = 128
NGROUP, PER_GROUP = 4, 8
NEXP = NGROUP * PER_GROUP
HID = 256
PLE = 256
EPS = 1e-6
BLK = 64
M_AT = (0, 4 * P, 7 * P, 9 * P)
CM_CREDIT = 4
CONV_STEPS = CONV_K + 2 * MCONV_K
MAX_OVER = (2 * SEQ - NEXP) // BLK
NBLK = 48
OUT_OF_RANGE = 4096
BIG = 1e30
RING = 4
Q0, K0, V0, CONV0, MQ0, MK0, MV0, MO0, IF0, GATE0 = (
    0, 1536, 2048, 2560, 3584, 4096, 4608, 5120, 5632, 5640)

_C = {}
_at = 0
for _name, _n in (("ident", P), ("upper", P), ("ones", P), ("mean", P), ("causal", P),
                  ("dist4", SEQ), ("dist16", SEQ), ("dist1", 2 * P), ("sel", 4 * P), ("rev32", NEXP),
                  ("iota32", NEXP), ("rev4", NGROUP), ("limit", 7), ("iota15", MAX_OVER),
                  ("slope", 3 * SLOTS), ("token", 2 * T), ("row", 2 * T)):
    _C[_name] = (_at, _n)
    _at += _n
NCONST = _at
G_MIX, G_FFN, G_PLE, CONV_W, CONV_B, LN_G, LN_B, MCONV, EPS_COL, NCHAN = (
    0, 8, 16, 24, 148, 152, 156, 160, 200, 201)


def constants():
    c = np.zeros((P, NCONST), np.float32)

    def put(name, value):
        at, n = _C[name]
        c[:, at:at + n] = value

    row, col = np.arange(P)[:, None], np.arange(P)[None, :]
    put("ident", row == col)
    put("upper", row < col)
    put("ones", 1.0)
    put("mean", 1.0 / CH)
    put("causal", np.where(row > col, BIG, 0.0))
    for name, dil, blocks in (("dist1", 1, 2), ("dist4", 4, 4), ("dist16", 16, 4)):
        d = row + (blocks - 1) * P - np.arange(blocks * P)[None, :]
        ok = (d >= 0) & (d % dil == 0) & (d <= dil * STEPS)
        put(name, np.where(ok, -d, -BIG))
    sel = np.zeros((P, 4, P))
    for h in range(4):
        sel[h, h] = 1.0
    put("sel", sel.reshape(P, 4 * P))
    put("rev32", NEXP - np.arange(NEXP)[None])
    put("iota32", np.arange(NEXP)[None])
    put("rev4", NGROUP - np.arange(NGROUP)[None])
    put("limit", BLK * np.arange(1, 8)[None])
    put("iota15", np.arange(MAX_OVER)[None])
    j = np.arange(1, 3 * SLOTS + 1, dtype=np.float32)
    slopes = (np.float32(2.0) ** (-np.float32(8.0) * j / np.float32(24))).reshape(3, SLOTS // 2, 2)
    put("slope", slopes.transpose(1, 2, 0).reshape(1, -1))
    k, t = np.divmod(np.arange(2 * T), T)
    put("token", t[None] * P + row)
    put("row", k[None] * SEQ + t[None] * P + row)
    return c


def build(nc, x, consts, chan, if_bias, r_bias, g_final, w_cm, w_tm, w_if, w_gate, w_branch, w_out,
          w_router, w_expert, w_pg, w_pp, pT, out):
    normed = nc.dram_tensor("normed", [SEQ, D], F32, kind="Internal").ap()
    expert_rows = nc.dram_tensor("expert_rows", [2 * SEQ, D], F32, kind="Internal").ap()
    table_dram = nc.dram_tensor("table_dram", [BLK * NBLK, 4], I32, kind="Internal").ap()

    with ExitStack() as ctx:
        def sb(name, shape, dt=F32):
            return ctx.enter_context(nc.sbuf_tensor(name, shape, dt))

        def sem(name):
            return ctx.enter_context(nc.semaphore(name))

        x_sb = sb("x_sb", [P, T, D])
        hT = sb("hT", [P, KD, SEQ])
        mT = sb("mT", [P, KD, SEQ])
        cst = sb("cst", [P, NCONST])
        chn = sb("chn", [P, NCHAN])
        yT = sb("yT", [P, 3, ROUNDS, SEQ])
        arena = sb("arena", [P, 116 * 256])
        if_b = sb("if_b", [P, 8])
        r_b = sb("r_b", [P, 36])
        small = sb("small", [P, 96])
        banks = [ctx.enter_context(nc.psum_tensor(f"bank{i}", [P, 512], F32)) for i in range(8)]
        PA, PB, S_1, S_4, S_16, TR, OUT, MM = banks

        def const(name, rows=P):
            at, n = _C[name]
            return cst[0:rows, at:at + n]

        ident, ones = const("ident"), const("ones")

        class Place:

            def __init__(self, kib):
                self.at = int(kib * 256)

            def take(self, *shape):
                n = int(np.prod(shape))
                piece = arena[:, self.at:self.at + n]
                self.at += n
                assert self.at <= 116 * 256
                names = "abc"[:len(shape)]
                if len(shape) > 1:
                    piece = piece.rearrange(f"p ({' '.join(names)}) -> p {' '.join(names)}",
                                            **dict(zip(names, shape)))
                return piece

        pl = Place(0)
        bias = pl.take(2, 1280)
        bias_flat = arena[:, 0:2560]
        sc = pl.take(2, 1280)
        psm = pl.take(2, SEQ)
        pT_sb = pl.take(2, SEQ)
        oatt = pl.take(T, P)
        ypad = pl.take(CONV_K - 1 + SEQ)
        cacc = pl.take(2, SEQ)
        sgt = pl.take(SEQ)
        qT = pl.take(3, SEQ)
        kT = pl.take(SEQ)
        gone = pl.at
        wcm = Place(48).take(4, KD * P)
        wtm = Place(64).take(KD, 3 * P)
        assert gone <= 48 * 256, gone
        pl = Place(76)
        tmv = pl.take(T, 3 * P + 1)
        raw = pl.take(2, MCONV_K - 1 + SEQ)
        qk = pl.take(2, SEQ)
        sqk = pl.take(2, SEQ)
        mb = pl.take(4, SEQ)
        mbd = sqk[:, 0, :]
        wm = pl.take(1280)
        wms = wm
        ym = pl.take(T, P)
        sgo = sgt.rearrange("p (t c) -> p t c", t=T)
        rows = Place(20).take(5, SEQ)
        wg = [Place(48).take(3, KD * P), Place(66).take(3, KD * P)]
        wb = [Place(60).take(3, 4 * P), Place(78).take(3, 4 * P)]
        wo = Place(84).take(KD, D)
        pl = Place(84)
        lnt = pl.take(ROUNDS, SEQ)
        sgl = pl.take(ROUNDS, SEQ)
        rst = pl.take(SEQ)
        lnr = pl.take(SEQ)
        pl = Place(24)
        sgm = pl.take(3, SEQ)
        mp = pl.take(3, SEQ)
        we = [Place(24 * b).take(6144) for b in range(RING)]
        yflat = yT[:, :, :, :].rearrange("p b r s -> p (b r s)")
        n2 = yflat[:, 0:T * D].rearrange("p (t d) -> p t d", t=T)
        pple = n2
        xT = [yflat[:, 4096 + b * 512:4608 + b * 512].rearrange("p (k s) -> p k s", k=KD) for b in range(2)]
        hx = yflat[:, 5120:5248].rearrange("p (j s) -> p j s", j=2)
        sgx = yflat[:, 5248:5376].rearrange("p (j s) -> p j s", j=2)
        pl = Place(96)
        p_in = pl.take(2, SEQ)
        pple_w = pl.take(2, D)
        junk1, junk2, junk3 = bias_flat[:, 0:D], Place(78).take(D), Place(72).take(D)
        sg6 = Place(76).take(D)
        pl = Place(96)
        yk = pl.take(2, 2, D)
        gfin_sb = pl.take(D)
        mT_tok = mT[:, :, :].rearrange("p k s -> p (k s)").rearrange("p (t d) -> p t d", t=T)
        n3 = mT_tok
        mflat = mT[:, :, :].rearrange("p k s -> p (k s)")
        xr = [mflat[0:BLK, b * D:(b + 1) * D] for b in range(2)]
        yr = [mflat[0:BLK, (2 + b) * D:(3 + b) * D] for b in range(2)]
        wr_sb = sb("wr_sb", [P, KD, 36])
        rl = sb("rl", [P, T, 36])
        le = sb("le", [P, T, NEXP])
        oh = sb("oh", [P, 2, T, NEXP])
        tmp = sb("tmp", [P, 8, NEXP])
        oh4 = sb("oh4", [P, T, NGROUP])
        t4 = sb("t4", [P, T, NGROUP])
        cc = sb("cc", [P, T + 1, NEXP])
        ov = sb("ov", [P, 3, NEXP])
        per = sb("per", [P, 12, 2, T])
        info = sb("info", [P, 2 * T, 4], I32)
        where = sb("where", [P, 2 * T], I32)
        ctl = sb("ctl", [1, 16], I32)
        ctlf = sb("ctlf", [1, 16])
        table = sb("table", [BLK, NBLK, 4], I32)
        gidx = sb("gidx", [BLK, 2, 2], I32)
        sidx = sb("sidx", [BLK, 2, 2], I32)
        over_cmp = mflat[:, 3072:3296].rearrange("p (e m) -> p e m", m=7)
        over_ids = mflat[0:1, 2048:2048 + MAX_OVER * NEXP].rearrange("p (b e) -> p b e", e=NEXP)

        def table_w(col):
            return table[:, bass.ds(col, 1), 2:3].rearrange("p a b -> p (a b)").bitcast(F32)

        ss, rr, ss2, rr2, ss3, rr3, ss4, rr4 = (small[:, 4 * i:4 * i + 4] for i in range(8))
        mx3 = small[:, 32:38].rearrange("p (b g) -> p b g", b=2)
        nmx = small[:, 38:40]
        den = small[:, 40:48]
        rden = small[:, 48:56]
        ucol = sb("ucol", [P, T, 4])
        ecol = sb("ecol", [P, T, 4])
        slope_now = sb("slope_now", [P, 6])
        md = sb("md", [P, 2, T])
        ifs = sb("ifs", [P, T, 8])
        lft = sb("lft", [P, 3, T, 4])

        x_loaded = [sem(f"x_loaded{t}") for t in range(T)]
        params_loaded = sem("params_loaded")
        ready = sem("ready")
        x_squared = sem("x_squared")
        rooted = sem("rooted")
        ln_root = sem("ln_root")
        dve_step = sem("dve_step")
        act_step = sem("act_step")
        x_normed = sem("x_normed")
        x_turned = sem("x_turned")
        h_ready = sem("h_ready")
        if_projected = sem("if_projected")
        if_ready = sem("if_ready")
        lf_ready = sem("lf_ready")
        if_turned = sem("if_turned")
        prefix_ready = sem("prefix_ready")
        em_ready = sem("em_ready")
        max_spread = sem("max_spread")
        cols_turned = sem("cols_turned")
        mb_ready = sem("mb_ready")
        cm_loaded = [sem(f"cm_loaded{s}") for s in range(4)]
        cm_done = sem("cm_done")
        tm_loaded = sem("tm_loaded")
        tm_done = sem("tm_done")
        bank_read = [sem("bank_a_read"), sem("bank_b_read")]
        conv_step = sem("conv_step")
        conv_ready = sem("conv_ready")
        mq_sig = sem("mq_sig")
        qk_ready = sem("qk_ready")
        slope_ready = sem("slope_ready")
        bias_ready = sem("bias_ready")
        mbd_ready = sem("mbd_ready")
        scores_done = sem("scores_done")
        biased = sem("biased")
        negmax_ready = sem("negmax_ready")
        exps_done = sem("exps_done")
        pool_step = sem("pool_step")
        probs_ready = sem("probs_ready")
        probs_turned = sem("probs_turned")
        pt_ready = sem("pt_ready")
        pv_done = sem("pv_done")
        rden_ready = sem("rden_ready")
        att_out = sem("att_out")
        att_turned = sem("att_turned")
        m_scores = sem("m_scores")
        m_weights = sem("m_weights")
        m_weighted = sem("m_weighted")
        m_num = sem("m_num")
        sgo_ready = sem("sgo_ready")
        md_step = sem("md_step")
        ym_ready = sem("ym_ready")
        ym_turned = sem("ym_turned")
        y_ready = sem("y_ready")
        ln_mm = sem("ln_mm")
        ln_step = sem("ln_step")
        ln_act = sem("ln_act")
        yconv_ready = sem("yconv_ready")
        mw_loaded = [sem("mw_loaded0"), sem("mw_loaded1")]
        gate_done = sem("gate_done")
        branch_done = sem("branch_done")
        gate_read = sem("gate_read")
        branch_read = sem("branch_read")
        merge_step = sem("merge_step")
        merged = sem("merged")
        wo_loaded = sem("wo_loaded")
        x2_mm = sem("x2_mm")
        x2_ready = sem("x2_ready")
        x2_squared = sem("x2_squared")
        n2_ready = sem("n2_ready")
        n2_stored = sem("n2_stored")
        n2_turned = sem("n2_turned")
        h2_ready = sem("h2_ready")
        logits_done = sem("logits_done")
        group_exp = sem("group_exp")
        pair_exp = sem("pair_exp")
        shifted = sem("shifted")
        diff_ready = sem("diff_ready")
        onehots = sem("onehots")
        counts_done = sem("counts_done")
        routed = sem("routed")
        table_blank = sem("table_blank")
        table_written = sem("table_written")
        table_loaded = sem("table_loaded")
        pw_loaded = sem("pw_loaded")
        ple_mm = sem("ple_mm")
        ple_copied = sem("ple_copied")
        we_loaded = [sem(f"we_loaded{b}") for b in range(RING)]
        idx_copied = sem("idx_copied")
        rows_gathered = [sem("rows_gathered0"), sem("rows_gathered1")]
        rows_turned = sem("rows_turned")
        xT_ready = sem("xT_ready")
        gu_done = sem("gu_done")
        gate_sig = sem("gate_sig")
        gate_mul = sem("gate_mul")
        hx_ready = sem("hx_ready")
        down_done = sem("down_done")
        y_low = sem("y_low")
        y_high = sem("y_high")
        rows_scattered = [sem("rows_scattered0"), sem("rows_scattered1")]
        ov_w = sem("ov_w")
        ov_gathered = sem("ov_gathered")
        ov_scattered = sem("ov_scattered")
        ov_all = sem("ov_all")
        rows_loaded = [sem("rows_loaded0"), sem("rows_loaded1")]
        pg_loaded = sem("pg_loaded")
        x3_ready = sem("x3_ready")
        x3_squared = sem("x3_squared")
        n3_ready = sem("n3_ready")
        n3_turned = sem("n3_turned")
        h3_ready = sem("h3_ready")
        pg_mm = sem("pg_mm")
        pg_sig = sem("pg_sig")
        x4_ready = sem("x4_ready")
        x4_squared = sem("x4_squared")
        out_ready = sem("out_ready")
        stored = sem("stored")

        N_PARAMS = 6

        CM_ORDER = 8
        takes_wait = sb("takes_wait", [1, 4])

        block = ctx.enter_context(nc.Block())

        @block.sync
        def _(sp):
            for t in range(T):
                sp.dma_start(x_sb[:, t, :], x[t * P:(t + 1) * P, :]).then_inc(x_loaded[t], 16)
            for dst, src in ((cst[:, :], consts), (chn[:, :], chan),
                             (if_b[:, :], if_bias.partition_broadcast(P)),
                             (r_b[:, :], r_bias.partition_broadcast(P)),
                             (wr_sb[:, :, :], w_router),
                             (wtm[:, 0, 0:KD * 8], w_if)):
                sp.dma_start(dst, src).then_inc(params_loaded, 16)

            with sp.Fori(0, ROUNDS) as r:
                for n in range(CM_ORDER):
                    sp.wait_ge(cm_done, r * CM_ORDER + n + 1)
                    sp.dma_start(wcm[:, n % 4, :], w_cm[r, n, :, :]).then_inc(cm_loaded[n % 4], 16)
                    if n == 3:
                        sp.wait_ge(if_projected, 1)
                        sp.wait_ge(tm_done, r * T)
                        sp.dma_start(wtm, w_tm[r, :, :, :]).then_inc(tm_loaded, 16)

            def merge_weights(slot, dt):
                sp.dma_start(wg[slot], w_gate[dt, :, :, :]).then_inc(mw_loaded[slot], 16)
                sp.dma_start(wb[slot], w_branch[dt, :, :, :]).then_inc(mw_loaded[slot], 16)

            sp.wait_ge(cm_done, CM_CREDIT + ROUNDS * CM_ORDER)
            sp.wait_ge(tm_done, ROUNDS * T)
            merge_weights(0, 0)
            sp.wait_ge(y_ready, 2 * ROUNDS)
            merge_weights(1, 1)

            def expert_weights(b, e):
                sp.dma_start(we[b], w_expert[e, :, :]).then_inc(we_loaded[b], 16)

            expert_weights(0, 0)
            sp.wait_ge(yconv_ready, ROUNDS)
            sp.dma_start(wo, w_out).then_inc(wo_loaded, 16)

            with sp.Fori(0, KD // 2 - 1) as i:
                for s in range(2):
                    sp.wait_ge(branch_done, 3 * (2 * i + s + 1))
                    merge_weights(s, 2 * i + s + 2)
            sp.wait_ge(merged, KD)
            expert_weights(1, 1)
            expert_weights(2, 2)
            for t in range(T):
                sp.wait_ge(n2_ready, t + 1)
                sp.dma_start(normed[t * P:(t + 1) * P, :], n2[:, t, :]).then_inc(n2_stored, 16)
            sp.wait_ge(x2_mm, 2 * T)
            sp.wait_ge(x2_squared, T)
            sp.dma_start(pple_w, w_pp).then_inc(pw_loaded, 16)
            sp.dma_start(p_in, pT).then_inc(pw_loaded, 16)
            expert_weights(3, 3)
            sp.wait_ge(table_written, 2 * T * 16)
            sp.dma_start(table[:, :, :], table_dram.rearrange("(j b) w -> j b w", b=NBLK)).then_inc(table_loaded, 16)
            with sp.Fori(0, NEXP // RING - 1) as i:
                for b in range(RING):
                    sp.wait_ge(down_done, 2 * (RING * i + b + 1))
                    expert_weights(b, RING * (i + 1) + b)
            for half in range(2):
                sp.wait_ge(down_done, 2 * (NEXP - RING + half + 1))
                sp.dma_start(we[half][:, 0:4096], w_pg[half, :, :]).then_inc(pg_loaded, 16)
            sp.wait_ge(down_done, 2 * NEXP)
            sp.wait_ge(routed, 2)
            n_over = sp.value_load(ctl[0:1, 0:1], min_val=0, max_val=MAX_OVER)
            with sp.Fori(0, MAX_OVER) as j:
                with sp.If(j < n_over):
                    sp.wait_ge(down_done, 2 * (NEXP + j))
                    e = sp.value_load(ctl[0:1, bass.ds(j + 1, 1)], min_val=0, max_val=NEXP - 1)
                    sp.dma_start(we[3], w_expert[e, :, :]).then_inc(ov_w, 16)

            sp.wait_ge(ov_all, 1)
            sp.dma_start(gfin_sb, g_final.partition_broadcast(P)).then_inc(pg_loaded, 16)
            for t in range(T):
                if t >= 2:
                    sp.wait_ge(x3_ready, t - 1)
                for k in range(2):
                    sp.dma_start(yk[:, t % 2, k, :],
                                 expert_rows[k * SEQ + t * P:k * SEQ + (t + 1) * P, :]).then_inc(rows_loaded[t % 2], 16)
            for t in range(T):
                sp.wait_ge(out_ready, t + 1)
                sp.dma_start(out[t * P:(t + 1) * P, :], x_sb[:, t, :]).then_inc(stored, 16)
            sp.wait_ge(stored, T * 16)

        @block.scalar
        def _(act):
            roots = [0]

            def root(dst, total, squared, count):
                roots[0] += 1
                act.wait_ge(squared, count)
                act.activation(dst, total, ACT.Sqrt, scale=1.0 / D, bias=chn[:, EPS_COL:EPS_COL + 1]).then_inc(rooted, 1)

            for t in range(T):
                act.wait_ge(x_loaded[t], 16)
                if t:
                    act.wait_ge(x_squared, t)
                act.activation(junk1, x_sb[:, t, :], ACT.Square, accum_out=ss[:, t:t + 1]).then_inc(x_squared, 1)
            act.wait_ge(params_loaded, N_PARAMS * 16)
            for t in range(T):
                root(rr[:, t:t + 1], ss[:, t:t + 1], x_squared, t + 1)
            act.wait_ge(if_ready, 1)
            act.activation(lft[:, 0], ifs[:, :, 4:8], ACT.Abs).then_inc(act_step, 1)
            act.wait_ge(act_step, 1)
            act.activation(lft[:, 1], lft[:, 0], ACT.Exp, scale=-1.0).then_inc(act_step, 1)
            act.wait_ge(act_step, 2)
            act.activation(lft[:, 2], lft[:, 1], ACT.Ln, bias=1.0).then_inc(act_step, 1)
            act.wait_ge(prefix_ready, 5)
            act.activation(rows[0:4, 4, :], rows[0:4, 3, :], ACT.Exp, scale=-1.0).then_inc(em_ready, 1)

            with act.Fori(0, ROUNDS) as r:
                def unit(u):
                    return r * 8 + u + 1

                act.wait_ge(cm_done, CM_CREDIT + r * CM_ORDER + 1)
                act.activation(sgt, PA[:, :], ACT.Sigmoid).then_inc(bank_read[0], 1)
                for n, dst, scale in ((2, raw[:, 0, MCONV_K - 1:], 1.0), (3, raw[:, 1, MCONV_K - 1:], 1.0),
                                      (4, qT[:, 0], HEAD ** -0.5), (5, qT[:, 1], HEAD ** -0.5),
                                      (6, qT[:, 2], HEAD ** -0.5), (7, kT, 1.0)):
                    act.wait_ge(cm_done, CM_CREDIT + r * CM_ORDER + n + 1)
                    act.activation(dst, (PA, PB)[n % 2][:, :], ACT.Copy, scale=scale).then_inc(bank_read[n % 2], 1)
                for c in range(2):
                    act.wait_ge(conv_step, r * CONV_STEPS + CONV_K + 4 * (c + 1))
                    act.activation(sqk[:, c], qk[:, c], ACT.Sigmoid).then_inc(mq_sig, 1)

                def pt_copy(u):
                    n = (u % 4 + 1) * P
                    act.wait_ge(probs_turned, unit(u))
                    act.activation(pT_sb[:, u % 2, 0:n], TR[:, 0:n], ACT.Copy).then_inc(pt_ready, 1)

                for u in range(8):
                    i = u % 4
                    n = min(i + 1, 2) * P + 2 * (i + 1) * P
                    act.wait_ge(negmax_ready, unit(u))
                    act.activation(sc[:, u % 2, 0:n], sc[:, u % 2, 0:n], ACT.Exp, bias=nmx[:, u % 2:u % 2 + 1],
                                   accum_out=den[:, u:u + 1]).then_inc(exps_done, 1)
                    if u < T:
                        act.wait_ge(tm_done, r * T + u + 1)
                        act.activation(tmv[:, u, 0:3 * P], (PA, PB)[u % 2][:, 0:3 * P], ACT.Copy)\
                           .then_inc(bank_read[u % 2], 1)
                    if u >= 1:
                        pt_copy(u - 1)
                    if 2 <= u < 6:
                        j = u - 2
                        at, width = M_AT[j], (T - j) * P
                        act.wait_ge(mbd_ready, r + 1)
                        act.activation(wm[:, at:at + P], mbd[:, j * P:(j + 1) * P], ACT.Exp,
                                       bias=ucol[:, j, bass.ds(r, 1)], scale=-1.0).then_inc(m_weights, 1)
                        if j < T - 1:
                            act.activation(wm[:, at + P:at + width], mb[:, bass.ds(r, 1), (j + 1) * P:], ACT.Exp,
                                           bias=ucol[:, j, bass.ds(r, 1)], scale=-1.0).then_inc(m_weights, 1)
                act.activation(sgo, tmv[:, :, P:2 * P], ACT.Sigmoid).then_inc(sgo_ready, 1)
                pt_copy(7)
                act.wait_ge(att_turned, r + 1)
                act.activation(yT[:, 0, bass.ds(r, 1), :], TR[:, :], ACT.Copy).then_inc(y_ready, 1)
                act.wait_ge(ym_turned, r + 1)
                act.activation(yT[:, 1, bass.ds(r, 1), :], MM[:, :], ACT.Copy).then_inc(y_ready, 1)

            act.wait_ge(ln_step, 4)
            for c in range(ROUNDS):
                act.activation(lnt[:, c], yT[:, 2, c, :], ACT.Square).then_inc(ln_act, 1)
            act.wait_ge(ln_step, 5)
            act.activation(lnr, rst, ACT.Sqrt).then_inc(ln_root, 1)
            for c in range(ROUNDS):
                act.wait_ge(ln_step, 6 + c)
                act.activation(sgl[:, c], yT[:, 2, c, :], ACT.Sigmoid, scale=chn[:, LN_G + c:LN_G + c + 1],
                               bias=chn[:, LN_B + c:LN_B + c + 1]).then_inc(ln_act, 1)
            act.sem_inc(gate_read, 3)
            with act.Fori(0, KD) as dt:
                for br in range(3):
                    act.wait_ge(gate_done, dt * 3 + br + 1)
                    act.wait_ge(merged, dt)
                    act.activation(sgm[:, br], (PA, S_1, S_16)[br][:, :], ACT.Sigmoid).then_inc(gate_read, 1)

            for t in range(T):
                act.wait_ge(x2_ready, 2 * (t + 1))
                if t:
                    act.wait_ge(x2_squared, t)
                act.activation(junk2, x_sb[:, t, :], ACT.Square, accum_out=ss2[:, t:t + 1]).then_inc(x2_squared, 1)
                root(rr2[:, t:t + 1], ss2[:, t:t + 1], x2_squared, t + 1)
            act.wait_ge(shifted, 1)
            act.activation(t4[:, :, :], t4[:, :, :], ACT.Exp).then_inc(group_exp, 1)
            act.wait_ge(diff_ready, 1)
            act.activation(per[:, 0, 0, :], per[:, 0, 1, :], ACT.Exp).then_inc(pair_exp, 1)
            for t in range(T):
                act.wait_ge(ple_mm, 2 * (t + 1))
                for half in range(2):
                    act.activation(pple[:, t, half * 512:(half + 1) * 512], (PA, PB, S_1, S_4)[(2 * t + half) % 4][:, :],
                                   ACT.Copy).then_inc(ple_copied, 1)

            def expert(n, b2, col, first_wait):
                act.wait_ge(gu_done, n + 1)
                act.activation(sgx, MM[:, 0:2 * BLK], ACT.Sigmoid).then_inc(gate_sig, 1)
                act.wait_ge(down_done, 2 * n + 1)
                first_wait()
                act.activation(yr[b2][:, 0:512], OUT[0:BLK, :], ACT.Copy,
                               scale=table_w(col)).then_inc(y_low, 1)

            act.wait_ge(table_loaded, 16)
            with act.Fori(0, NEXP // RING) as i:
                for b in range(RING):
                    expert(RING * i + b, b % 2, RING * i + b,
                           lambda b=b: act.wait_ge(rows_scattered[b % 2], (2 * i + b // 2) * 16))
            for b in range(2):
                act.wait_ge(rows_scattered[b], NEXP // 2 * 16)
            act.wait_ge(routed, 2)
            n_over = act.value_load(ctl[0:1, 0:1], min_val=0, max_val=MAX_OVER)
            with act.Fori(0, MAX_OVER) as j:
                with act.If(j < n_over):
                    expert(NEXP + j, 0, NEXP + j, lambda: act.wait_ge(ov_scattered, j * 16))

            def x3_scale(t):
                act.wait_ge(x3_ready, t + 1)
                if t:
                    act.wait_ge(x3_squared, t)
                act.activation(junk3, x_sb[:, t, :], ACT.Square, accum_out=ss3[:, t:t + 1]).then_inc(x3_squared, 1)
                root(rr3[:, t:t + 1], ss3[:, t:t + 1], x3_squared, t + 1)

            x3_scale(0)
            for t in range(T):
                for half in range(2):
                    act.wait_ge(pg_mm, 2 * t + half + 1)
                    if t:
                        act.wait_ge(x4_squared, t)
                    act.activation(sg6[:, half * 512:(half + 1) * 512], (PA, PB, S_1, S_4)[(2 * t + half) % 4][:, :],
                                   ACT.Sigmoid).then_inc(pg_sig, 1)
                    if half == 0 and t + 1 < T:
                        x3_scale(t + 1)
                act.wait_ge(x4_ready, t + 1)
                act.activation(sg6, x_sb[:, t, :], ACT.Square, accum_out=ss4[:, t:t + 1]).then_inc(x4_squared, 1)
                root(rr4[:, t:t + 1], ss4[:, t:t + 1], x4_squared, t + 1)

        @block.tensor
        def _(pe):
            def mm(out, lhsT, rhs, start=True, stop=True):
                return pe.matmul(out, lhsT, rhs, start=start, stop=stop)

            pe.sem_inc(cm_done, CM_CREDIT)
            pe.wait_ge(params_loaded, N_PARAMS * 16)
            for t in range(T):
                pe.wait_ge(x_normed, t + 1)
                for half in range(2):
                    if t:
                        pe.wait_ge(h_ready, 2 * t + half - 1)
                    for k in range(4):
                        last = pe.transpose((PA, PB)[half][:, k * P:(k + 1) * P],
                                            mT_tok[:, t, (4 * half + k) * P:(4 * half + k + 1) * P], ident)
                    last.then_inc(x_turned, 1)
            pe.wait_ge(h_ready, 2 * T)
            for t in range(T):
                for k in range(KD):
                    last = mm(MM[:, t * 8:t * 8 + 8], hT[:, k, t * P:(t + 1) * P], wtm[:, 0, k * 8:k * 8 + 8],
                              k == 0, k == KD - 1)
            last.then_inc(if_projected, 1)
            pe.wait_ge(if_ready, 1)
            for t in range(T):
                pe.transpose(S_1[0:4, t * P:(t + 1) * P], ifs[:, t, 0:4], ident)
            pe.wait_ge(lf_ready, 1)
            for t in range(T):
                last = pe.transpose(S_4[0:4, t * P:(t + 1) * P], lft[:, 0, t, :], ident)
            last.then_inc(if_turned, 1)
            pe.wait_ge(prefix_ready, 4)
            for h in range(4):
                last = mm((PA, PB, S_16, OUT)[h][:, :], const("sel", 4)[:, h * P:(h + 1) * P], rows[0:4, 2, :])
            last.then_inc(max_spread, 1)
            pe.wait_ge(em_ready, 1)
            for q, row in enumerate((1, 4)):
                for t in range(T):
                    last = pe.transpose(TR[:, (q * T + t) * 4:(q * T + t) * 4 + 4],
                                        rows[0:4, row, t * P:(t + 1) * P], ident[0:4, 0:4])
            last.then_inc(cols_turned, 1)
            pe.wait_ge(mb_ready, 5)

            with pe.Fori(0, ROUNDS) as r:
                def unit(u):
                    return r * 8 + u + 1

                for n in range(CM_ORDER):
                    pe.wait_ge(cm_loaded[n % 4], (2 * r + n // 4 + 1) * 16)
                    pe.wait_ge(bank_read[n % 2], 6 * r + n // 2)
                    for k in range(KD):
                        last = mm((PA, PB)[n % 2][:, :], wcm[:, n % 4, k * P:(k + 1) * P], hT[:, k, :],
                                  k == 0, k == KD - 1)
                    last.then_inc(cm_done, 1)

                def scores(u):
                    s, i = divmod(u, 4)
                    if u:
                        pe.wait_ge(negmax_ready, unit(u - 1))
                    lo, hi = s * HEAD, (s + 1) * HEAD
                    for g, bank in enumerate((S_1, S_4, S_16)):
                        k0 = max(0, i - 1) * P if g == 0 else 0
                        n = (i + 1) * P - k0
                        last = mm(bank[:, 0:n], qT[lo:hi, g, i * P:(i + 1) * P], kT[lo:hi, k0:k0 + n])
                    last.then_inc(scores_done, 1)

                def turn(u):
                    pe.wait_ge(probs_ready, unit(u))
                    pe.wait_ge(pt_ready, r * 8 + u)
                    for j in range(u % 4 + 1):
                        last = pe.transpose(TR[:, j * P:(j + 1) * P], psm[:, u % 2, j * P:(j + 1) * P], ident)
                    last.then_inc(probs_turned, 1)

                def pv(u):
                    s, i = divmod(u, 4)
                    pe.wait_ge(pt_ready, unit(u))
                    if i == 0:
                        pe.wait_ge(att_out, 2 * r + s)
                    for j in range(i + 1):
                        last = mm(OUT[:, i * HEAD:(i + 1) * HEAD], pT_sb[:, u % 2, j * P:(j + 1) * P],
                                  tmv[:, j, s * HEAD:(s + 1) * HEAD], j == 0, j == i)
                    last.then_inc(pv_done, 1)

                for u in range(8):
                    if u == 0:
                        pe.wait_ge(bank_read[0], 6 * r + 4)
                        pe.wait_ge(bank_read[1], 6 * r + 4)
                    scores(u)
                    if u < T:
                        if u == 0:
                            pe.wait_ge(tm_loaded, (r + 1) * 16)
                        pe.wait_ge(bank_read[u % 2], 6 * r + 4 + u // 2)
                        for k in range(KD):
                            last = mm((PA, PB)[u % 2][:, 0:3 * P], hT[:, k, u * P:(u + 1) * P], wtm[:, k, :],
                                      k == 0, k == KD - 1)
                        last.then_inc(tm_done, 1)
                    else:
                        j = u - T
                        if j == 0:
                            pe.wait_ge(qk_ready, 2 * (r + 1))
                            pe.wait_ge(y_ready, 2 * r)
                        else:
                            pe.wait_ge(m_weighted, r * T + j)
                        mm(MM[:, 0:(T - j) * P], qk[:, 1, j * P:(j + 1) * P], qk[:, 0, j * P:]).then_inc(m_scores, 1)
                    if u >= 2:
                        pv(u - 2)
                    if u >= 1:
                        turn(u - 1)
                pe.wait_ge(negmax_ready, unit(7))
                pe.wait_ge(m_weighted, (r + 1) * T)
                for i in range(T):
                    bank, at = (S_1, S_4)[i // 2], (i % 2) * (DH + 1)
                    for j in range(i + 1):
                        q0 = M_AT[j] + (i - j) * P
                        last = mm(bank[:, at:at + DH + 1], wms[:, q0:q0 + P], tmv[:, j, 2 * P:3 * P + 1], j == 0, j == i)
                last.then_inc(m_num, 1)
                pv(6)
                turn(7)
                pv(7)
                pe.wait_ge(ym_ready, r + 1)
                for i in range(T):
                    last = pe.transpose(MM[:, i * P:(i + 1) * P], ym[:, i, :], ident)
                last.then_inc(ym_turned, 1)
                pe.wait_ge(att_out, 2 * r + 2)
                for i in range(T):
                    last = pe.transpose(TR[:, i * P:(i + 1) * P], oatt[:, i, :], ident)
                last.then_inc(att_turned, 1)
                pe.wait_ge(y_ready, 2 * r + 1)

            pe.wait_ge(conv_ready, ROUNDS)
            for b in range(2):
                pe.wait_ge(bank_read[b], 6 * ROUNDS)
            for c in range(ROUNDS):
                last = mm(PA[:, :], const("mean"), yT[:, 2, c, :], c == 0, c == ROUNDS - 1)
            last.then_inc(ln_mm, 1)
            pe.wait_ge(ln_act, ROUNDS)
            for c in range(ROUNDS):
                last = mm(PB[:, :], const("mean"), lnt[:, c, :], c == 0, c == ROUNDS - 1)
            last.then_inc(ln_mm, 1)
            pe.wait_ge(y_ready, 2 * ROUNDS)
            pe.wait_ge(ln_step, 5)
            with pe.Fori(0, KD // 2) as h:
                for s in range(2):
                    dt = 2 * h + s
                    pe.wait_ge(mw_loaded[s], (h + 1) * 32)
                    for br in range(3):
                        pe.wait_ge(gate_read, 3 * dt + br + 1)
                        for k in range(KD):
                            last = mm((PA, S_1, S_16)[br][:, :], wg[s][:, br, k * P:(k + 1) * P], hT[:, k, :],
                                      k == 0, k == KD - 1)
                        last.then_inc(gate_done, 1)
                        if s == 0 and br == 2:
                            pe.wait_ge(yconv_ready, ROUNDS)
                        pe.wait_ge(branch_read, 3 * dt + br + 1)
                        for k in range(4):
                            last = mm((PB, S_4, OUT)[br][:, :], wb[s][:, br, k * P:(k + 1) * P], yT[:, br, k, :],
                                      k == 0, k == 3)
                        last.then_inc(branch_done, 1)

            def project(t):
                for half in range(2):
                    n = 2 * t + half
                    if n >= 4:
                        pe.wait_ge(x2_ready, n - 3)
                    for k in range(KD):
                        last = mm((PA, PB, S_1, S_4)[n % 4][:, :], mT[:, k, t * P:(t + 1) * P],
                                  wo[:, k, half * 512:(half + 1) * 512], k == 0, k == KD - 1)
                    last.then_inc(x2_mm, 1)

            def turn_rows(t, source, rows_ready, done, read):
                pe.wait_ge(rows_ready, t + 1)
                for half in range(2):
                    if t:
                        pe.wait_ge(read, 2 * t + half - 1)
                    for k in range(4):
                        last = pe.transpose((S_16, OUT)[half][:, k * P:(k + 1) * P],
                                            source[:, t, (4 * half + k) * P:(4 * half + k + 1) * P], ident)
                    last.then_inc(done, 1)

            pe.wait_ge(wo_loaded, 16)
            pe.wait_ge(merged, KD)
            for t in range(T):
                project(t)
                if t:
                    turn_rows(t - 1, n2, n2_ready, n2_turned, h2_ready)
            turn_rows(T - 1, n2, n2_ready, n2_turned, h2_ready)
            pe.wait_ge(h2_ready, 2 * T)
            for t in range(T):
                for k in range(KD):
                    last = mm(MM[:, t * 36:(t + 1) * 36], hT[:, k, t * P:(t + 1) * P], wr_sb[:, k, :],
                              k == 0, k == KD - 1)
            last.then_inc(logits_done, 1)

            def ple(t):
                for half in range(2):
                    n = 2 * t + half
                    if n >= 4:
                        pe.wait_ge(ple_copied, n - 3)
                    for k in range(2):
                        last = mm((PA, PB, S_1, S_4)[n % 4][:, :], p_in[:, k, t * P:(t + 1) * P],
                                  pple_w[:, k, half * 512:(half + 1) * 512], k == 0, k == 1)
                    last.then_inc(ple_mm, 1)

            pe.wait_ge(pw_loaded, 32)
            pe.wait_ge(x2_ready, 2 * T)
            pe.wait_ge(n2_stored, T * 16)
            ple(0)
            ple(1)
            pe.wait_ge(onehots, 1)
            for t in range(T + 1):
                for q in range(min(t + 1, T)):
                    last = mm(TR[:, t * NEXP:(t + 1) * NEXP], const("upper") if q == t else ones, tmp[:, q, :],
                              q == 0, q == min(t, T - 1))
            last.then_inc(counts_done, 1)
            ple(2)
            ple(3)

            def turn_block(n, b2, gathered, value):
                pe.wait_ge(gathered, value)
                pe.wait_ge(xT_ready, n)
                for k in range(KD):
                    last = (pe.matmul if k == 0 else pe.transpose)(
                        TR[:, k * BLK:(k + 1) * BLK], xr[b2][:, k * P:(k + 1) * P], ident[0:BLK, 0:BLK],
                        **(dict(start=True, stop=True) if k == 0 else {}))
                last.then_inc(rows_turned, 1)

            def up(n, b2, w):
                pe.wait_ge(xT_ready, n + 1)
                for m in range(4):
                    for k in range(KD):
                        last = mm(MM[:, m * BLK:(m + 1) * BLK], w[:, k * 512 + m * P:k * 512 + (m + 1) * P],
                                  xT[b2][:, k, :], k == 0, k == KD - 1)
                last.then_inc(gu_done, 1)

            def down(n, w):
                pe.wait_ge(hx_ready, n + 1)
                pe.wait_ge(y_low, n)
                pe.wait_ge(y_high, n)
                for half in range(2):
                    for j in range(2):
                        at = 4096 + j * 1024 + half * 512
                        last = mm((OUT, S_16)[half][0:BLK, :], hx[:, j, :], w[:, at:at + 512], j == 0, j == 1)
                    last.then_inc(down_done, 1)

            pe.wait_ge(table_loaded, 16)
            turn_block(0, 0, rows_gathered[0], 16)
            with pe.Fori(0, NEXP // RING) as i:
                for b in range(RING):
                    n = RING * i + b
                    pe.wait_ge(we_loaded[b], (i + 1) * 16)
                    up(n, b % 2, we[b])
                    turn_block(n + 1, (b + 1) % 2, rows_gathered[(b + 1) % 2], (2 * i + (b + 1) // 2 + 1) * 16)
                    down(n, we[b])
            pe.wait_ge(routed, 2)
            n_over = pe.value_load(ctl[0:1, 0:1], min_val=0, max_val=MAX_OVER)
            with pe.Fori(0, MAX_OVER) as j:
                with pe.If(j < n_over):
                    turn_block(NEXP + 1 + j, 0, ov_gathered, (j + 1) * 16)
                    pe.wait_ge(ov_w, (j + 1) * 16)
                    pe.wait_ge(xT_ready, NEXP + 2 + j)
                    for m in range(4):
                        for k in range(KD):
                            last = mm(MM[:, m * BLK:(m + 1) * BLK], we[3][:, k * 512 + m * P:k * 512 + (m + 1) * P],
                                      xT[1][:, k, :], k == 0, k == KD - 1)
                    last.then_inc(gu_done, 1)
                    down(NEXP + j, we[3])

            pe.wait_ge(y_low, NEXP)
            pe.wait_ge(pg_loaded, 48)
            turn_rows(0, n3, n3_ready, n3_turned, h3_ready)
            for t in range(T):
                pe.wait_ge(h3_ready, 2 * (t + 1))
                for half in range(2):
                    n = 2 * t + half
                    if n >= 4:
                        pe.wait_ge(pg_sig, n - 3)
                    for k in range(KD):
                        last = mm((PA, PB, S_1, S_4)[n % 4][:, :], hT[:, k, t * P:(t + 1) * P],
                                  we[k // 4][:, (k % 4) * D + half * 512:(k % 4) * D + (half + 1) * 512],
                                  k == 0, k == KD - 1)
                    last.then_inc(pg_mm, 1)
                    if half == 0 and t + 1 < T:
                        turn_rows(t + 1, n3, n3_ready, n3_turned, h3_ready)

        @block.vector
        def _(dve):
            steps = [0]

            def chain(ins):
                steps[0] += 1
                ins.then_inc(dve_step, 1)
                dve.wait_ge(dve_step, steps[0])

            dve.memset(ypad[:, 0:CONV_K - 1], 0.0)
            dve.memset(raw[:, :, 0:MCONV_K - 1], 0.0)
            dve.memset(tmv[:, :, 3 * P:3 * P + 1], 1.0)
            chain(dve.memset(rows[0:4, 0, :], 1.0))
            dve.wait_ge(params_loaded, N_PARAMS * 16)

            def h_out(t, banks2, turned, gain, ready_sem):
                for half in range(2):
                    dve.wait_ge(turned, 2 * t + half + 1)
                    dve.tensor_tensor(hT[:, 4 * half:4 * half + 4, t * P:(t + 1) * P],
                                      banks2[half][:, :].rearrange("p (k s) -> p k s", k=4),
                                      chn[:, gain + 4 * half:gain + 4 * half + 4].unsqueeze(2).to_broadcast([P, 4, P]),
                                      ALU.mult).then_inc(ready_sem, 1)

            rooted_seen = [0]

            def rstd(root, total):
                rooted_seen[0] += 1
                dve.wait_ge(rooted, rooted_seen[0])
                chain(dve.tensor_scalar(total, total, 1.0 / D, EPS, ALU.mult, ALU.add))
                chain(dve.reciprocal(root, root))
                chain(dve.scalar_tensor_tensor(total, root, total, root, ALU.mult, ALU.mult))
                chain(dve.tensor_scalar(total, total, -0.5, 1.5, ALU.mult, ALU.add))
                chain(dve.tensor_tensor(root, root, total, ALU.mult))

            for t in range(T):
                rstd(rr[:, t:t + 1], ss[:, t:t + 1])
                dve.tensor_scalar(mT_tok[:, t, :], x_sb[:, t, :], rr[:, t:t + 1], None, ALU.mult).then_inc(x_normed, 1)
                if t:
                    h_out(t - 1, (PA, PB), x_turned, G_MIX, h_ready)
            h_out(T - 1, (PA, PB), x_turned, G_MIX, h_ready)

            dve.wait_ge(if_projected, 1)
            dve.tensor_tensor(ifs[:, :, :], MM[:, 0:32].rearrange("p (t c) -> p t c", t=T),
                              if_b[:, :].unsqueeze(1).to_broadcast([P, T, 8]), ALU.add).then_inc(if_ready, 1)
            dve.wait_ge(if_ready, 1)
            dve.wait_ge(act_step, 3)
            dve.scalar_tensor_tensor(lft[:, 0], ifs[:, :, 4:8], 0.0, lft[:, 2], ALU.min, ALU.subtract).then_inc(lf_ready, 1)
            dve.wait_ge(if_turned, 1)
            dve.tensor_tensor_scan(rows[0:4, 3, :], rows[0:4, 0, :], S_4[0:4, :], 0.0, ALU.mult, ALU.add).then_inc(prefix_ready, 1)
            dve.wait_ge(prefix_ready, 1)
            dve.tensor_tensor(rows[0:4, 1, :], S_1[0:4, :], rows[0:4, 3, :], ALU.subtract).then_inc(prefix_ready, 1)
            dve.wait_ge(prefix_ready, 2)
            dve.tensor_tensor_scan(rows[0:4, 2, :], rows[0:4, 1, :], rows[0:4, 1, :], 0.0, ALU.max, ALU.max).then_inc(prefix_ready, 2)
            dve.wait_ge(prefix_ready, 4)
            dve.tensor_tensor(rows[0:4, 3, :], rows[0:4, 3, :], rows[0:4, 2, :], ALU.add).then_inc(prefix_ready, 1)
            dve.wait_ge(max_spread, 1)
            for h in range(4):
                dve.tensor_copy(mb[:, h, :], (PA, PB, S_16, OUT)[h][:, :]).then_inc(mb_ready, 1)
            dve.wait_ge(cols_turned, 1)
            dve.tensor_copy(ucol[:, :, :], TR[:, 0:16].rearrange("p (t h) -> p t h", t=T))
            dve.tensor_copy(ecol[:, :, :], TR[:, 16:32].rearrange("p (t h) -> p t h", t=T)).then_inc(mb_ready, 1)
            dve.sem_inc(branch_read, 3)

            with dve.Fori(0, ROUNDS) as r:
                def unit(u):
                    return r * 8 + u + 1

                def conv(value):
                    dve.wait_ge(conv_step, r * CONV_STEPS + value)

                w31 = lambda j: chn[:, bass.ds(CONV_W + r * CONV_K + j, 1)]
                wq = lambda j: chn[:, bass.ds(MCONV + r * 10 + j, 1)]
                dve.wait_ge(bank_read[0], 6 * r + 1)
                dve.wait_ge(cm_done, CM_CREDIT + r * CM_ORDER + 2)
                dve.tensor_tensor(ypad[:, CONV_K - 1:], PB[:, :], sgt, ALU.mult).then_inc(bank_read[1], 1)
                dve.wait_ge(bank_read[1], 6 * r + 1)
                dve.tensor_scalar(cacc[:, 0], ypad[:, 0:SEQ], w31(0), chn[:, bass.ds(CONV_B + r, 1)],
                                  ALU.mult, ALU.add).then_inc(conv_step, 1)
                dve.tensor_scalar(cacc[:, 1], ypad[:, 1:1 + SEQ], w31(1), None, ALU.mult).then_inc(conv_step, 1)
                for j in range(2, CONV_K):
                    conv(j - 1)
                    dve.scalar_tensor_tensor(cacc[:, j % 2], ypad[:, j:j + SEQ], w31(j), cacc[:, j % 2],
                                             ALU.mult, ALU.add).then_inc(conv_step, 1)
                conv(CONV_K)
                dve.tensor_tensor(yT[:, 2, bass.ds(r, 1), :], cacc[:, 0], cacc[:, 1], ALU.add).then_inc(conv_ready, 1)
                dve.wait_ge(bank_read[0], 6 * r + 2)
                dve.wait_ge(bank_read[1], 6 * r + 2)
                for c in range(2):
                    dve.tensor_scalar(qk[:, c], raw[:, c, 0:SEQ], wq(4 * c), wq(8 + c), ALU.mult, ALU.add)\
                       .then_inc(conv_step, 1)
                    for j in range(1, MCONV_K):
                        conv(CONV_K + 4 * c + j)
                        dve.scalar_tensor_tensor(qk[:, c], raw[:, c, j:j + SEQ], wq(4 * c + j), qk[:, c],
                                                 ALU.mult, ALU.add).then_inc(conv_step, 1)
                for c in range(2):
                    dve.wait_ge(mq_sig, 2 * r + c + 1)
                    dve.scalar_tensor_tensor(qk[:, c], qk[:, c], 1.0 if c == 0 else DH ** -0.5, sqk[:, c],
                                             ALU.mult, ALU.mult).then_inc(qk_ready, 1)

                def out_of_slot(s):
                    dve.wait_ge(exps_done, unit(4 * s + 3))
                    dve.reciprocal(rden[:, 4 * s:4 * s + 4], den[:, 4 * s:4 * s + 4]).then_inc(rden_ready, 1)
                    dve.wait_ge(rden_ready, 2 * r + s + 1)
                    dve.wait_ge(pv_done, unit(4 * s + 3))
                    dve.tensor_tensor(oatt[:, :, s * HEAD:(s + 1) * HEAD],
                                      OUT[:, 0:T * HEAD].rearrange("p (i c) -> p i c", i=T),
                                      rden[:, 4 * s:4 * s + 4].unsqueeze(2).to_broadcast([P, T, HEAD]),
                                      ALU.mult).then_inc(att_out, 1)

                for u in range(8):
                    s, i = divmod(u, 4)
                    n, near = (i + 1) * P, min(i + 1, 2) * P
                    if u % 4 == 0:
                        dve.wait_ge(bias_ready, 6 * r + 3 * (s + 1))
                    if u >= 2:
                        dve.wait_ge(probs_ready, unit(u - 2))
                    dve.wait_ge(scores_done, unit(u))
                    dve.memset(takes_wait[:, 2:3], 0.0)
                    for g, (bank, at, width, b0) in enumerate(((S_4, 0, n, 512 - n), (S_16, n, n, 1024 - n),
                                                               (S_1, 2 * n, near, 1280 - near))):
                        dve.tensor_tensor_reduce(out=sc[:, u % 2, at:at + width], in0=bank[:, 0:width],
                                                 in1=bias[:, s, b0:b0 + width], scale=1.0, scalar=-3e38,
                                                 op0=ALU.add, op1=ALU.max,
                                                 accum_out=mx3[:, u % 2, g:g + 1]).then_inc(biased, 1)
                    dve.wait_ge(biased, 3 * unit(u))
                    dve.tensor_reduce(nmx[:, u % 2:u % 2 + 1], mx3[:, u % 2, :], AXX, ALU.max, negate=True)\
                       .then_inc(negmax_ready, 1)
                    if u >= T:
                        j = u - T
                        dve.wait_ge(m_scores, r * T + j + 1)
                        dve.wait_ge(m_weights, 7 * r + min(2 * (j + 1), 7))
                        at, width = M_AT[j], (T - j) * P
                        dve.tensor_tensor(wms[:, at:at + width], MM[:, 0:width], wm[:, at:at + width], ALU.mult)\
                           .then_inc(m_weighted, 1)
                    if u == 6:
                        out_of_slot(0)
                dve.wait_ge(m_num, r + 1)
                for q, bank in enumerate((S_1, S_4)):
                    dve.tensor_copy(md[:, 0, 2 * q:2 * q + 2].unsqueeze(2),
                                    bank[:, 0:2 * (DH + 1)].rearrange("p (i c) -> p i c", i=2)[:, :, DH:DH + 1])\
                       .then_inc(md_step, 1)
                dve.wait_ge(md_step, 5 * r + 2)
                dve.scalar_tensor_tensor(md[:, 1, :], md[:, 0, :], -1.0, md[:, 0, :], ALU.mult, ALU.max).then_inc(md_step, 1)
                dve.wait_ge(md_step, 5 * r + 3)
                dve.tensor_tensor(md[:, 1, :].unsqueeze(2), md[:, 1, :].unsqueeze(2), ecol[:, :, bass.ds(r, 1)], ALU.max)\
                   .then_inc(md_step, 1)
                dve.wait_ge(md_step, 5 * r + 4)
                dve.reciprocal(md[:, 1, :], md[:, 1, :]).then_inc(md_step, 1)
                dve.wait_ge(md_step, 5 * r + 5)
                dve.wait_ge(sgo_ready, r + 1)
                for i in range(T):
                    at = (i % 2) * (DH + 1)
                    last = dve.scalar_tensor_tensor(ym[:, i, :], (S_1, S_4)[i // 2][:, at:at + DH], md[:, 1, i:i + 1],
                                                    sgo[:, i, :], ALU.mult, ALU.mult)
                last.then_inc(ym_ready, 1)
                out_of_slot(1)

            dve.wait_ge(ln_mm, 1)
            for c in range(ROUNDS):
                dve.tensor_tensor(yT[:, 2, c, :], yT[:, 2, c, :], PA[:, :], ALU.subtract).then_inc(ln_step, 1)
            dve.wait_ge(ln_mm, 2)
            dve.tensor_scalar(rst, PB[:, :], EPS, None, ALU.add).then_inc(ln_step, 1)
            dve.wait_ge(ln_root, 1)
            chain(dve.reciprocal(lnr, lnr))
            chain(dve.tensor_tensor(rst, rst, lnr, ALU.mult))
            chain(dve.tensor_tensor(rst, rst, lnr, ALU.mult))
            chain(dve.tensor_scalar(rst, rst, -0.5, 1.5, ALU.mult, ALU.add))
            chain(dve.tensor_tensor(rst, rst, lnr, ALU.mult))
            for c in range(ROUNDS):
                dve.tensor_tensor(yT[:, 2, c, :], yT[:, 2, c, :], rst, ALU.mult).then_inc(ln_step, 1)
            for c in range(ROUNDS):
                dve.wait_ge(ln_step, 6 + c)
                dve.wait_ge(ln_act, 2 * ROUNDS - 3 + c)
                chain(dve.tensor_scalar(yT[:, 2, c, :], yT[:, 2, c, :], chn[:, LN_G + c:LN_G + c + 1],
                                        chn[:, LN_B + c:LN_B + c + 1], ALU.mult, ALU.add))
                dve.tensor_tensor(yT[:, 2, c, :], yT[:, 2, c, :], sgl[:, c], ALU.mult).then_inc(yconv_ready, 1)

            with dve.Fori(0, KD) as dt:
                for br in range(3):
                    dve.wait_ge(gate_read, 3 * dt + br + 4)
                    dve.wait_ge(branch_done, 3 * dt + br + 1)
                    dve.tensor_tensor(mp[:, br], (PB, S_4, OUT)[br][:, :], sgm[:, br], ALU.mult).then_inc(branch_read, 1)
                    if br == 1:
                        dve.wait_ge(branch_read, 3 * dt + 5)
                        dve.tensor_tensor(mp[:, 0], mp[:, 0], mp[:, 1], ALU.add).then_inc(merge_step, 1)
                dve.wait_ge(branch_read, 3 * dt + 6)
                dve.wait_ge(merge_step, dt + 1)
                dve.tensor_tensor(mT[:, bass.ds(dt, 1), :], mp[:, 0], mp[:, 2], ALU.add).then_inc(merged, 1)

            for t in range(T):
                for half in range(2):
                    dve.wait_ge(x2_mm, 2 * t + half + 1)
                    part = x_sb[:, t, half * 512:(half + 1) * 512]
                    dve.tensor_tensor(part, part, (PA, PB, S_1, S_4)[(2 * t + half) % 4][:, :], ALU.add).then_inc(x2_ready, 1)
                rstd(rr2[:, t:t + 1], ss2[:, t:t + 1])
                dve.tensor_scalar(n2[:, t, :], x_sb[:, t, :], rr2[:, t:t + 1], None, ALU.mult).then_inc(n2_ready, 1)
                if t:
                    h_out(t - 1, (S_16, OUT), n2_turned, G_FFN, h2_ready)
            h_out(T - 1, (S_16, OUT), n2_turned, G_FFN, h2_ready)

            def spread(ap, shape, axis):
                return ap.unsqueeze(axis).to_broadcast(shape)

            def first_max(onehot, value, rev, scratch, top, n):
                chain(dve.tensor_reduce(top, value, AXX, ALU.max))
                chain(dve.tensor_tensor(scratch, value, spread(top, [P, T, n], 2), ALU.is_equal))
                chain(dve.tensor_tensor(scratch, scratch, spread(rev, [P, T, n], 1), ALU.mult))
                chain(dve.tensor_reduce(per[:, 11, 0, :], scratch, AXX, ALU.max))
                chain(dve.tensor_tensor(onehot, scratch, spread(per[:, 11, 0, :], [P, T, n], 2), ALU.is_equal))

            dve.wait_ge(logits_done, 1)
            chain(dve.tensor_tensor(rl[:, :, :], MM[:, 0:T * 36].rearrange("p (t c) -> p t c", t=T),
                                    spread(r_b[:, :], [P, T, 36], 1), ALU.add))
            top_g, p_g, top_1, top_2 = (per[:, q, 0, :] for q in (1, 2, 3, 4))
            first_max(oh4[:, :, :], rl[:, :, 0:NGROUP], const("rev4"), t4[:, :, :], top_g, NGROUP)
            dve.tensor_tensor(t4[:, :, :], rl[:, :, 0:NGROUP], spread(top_g, [P, T, NGROUP], 2), ALU.subtract)\
               .then_inc(shifted, 1)
            chain(dve.tensor_scalar(oh4[:, :, :], oh4[:, :, :], 1.0, BIG, ALU.subtract, ALU.mult))
            chain(dve.tensor_tensor(le[:, :, :].rearrange("p t (g e) -> p t g e", g=NGROUP),
                                    rl[:, :, NGROUP:].rearrange("p t (g e) -> p t g e", g=NGROUP),
                                    spread(oh4[:, :, :], [P, T, NGROUP, PER_GROUP], 3), ALU.add))
            first_max(oh[:, 0], le[:, :, :], const("rev32"), tmp[:, 0:T, :], top_1, NEXP)
            chain(dve.scalar_tensor_tensor(le[:, :, :], oh[:, 0], -2 * BIG, le[:, :, :], ALU.mult, ALU.add))
            first_max(oh[:, 1], le[:, :, :], const("rev32"), tmp[:, 0:T, :], top_2, NEXP)
            dve.tensor_tensor(tmp[:, 0:T, :], oh[:, 0], oh[:, 1], ALU.add).then_inc(onehots, 1)
            dve.tensor_tensor(per[:, 0, 1, :], top_2, top_1, ALU.subtract).then_inc(diff_ready, 1)
            dve.wait_ge(group_exp, 1)
            chain(dve.tensor_reduce(p_g, t4[:, :, :], AXX, ALU.add))
            chain(dve.reciprocal(p_g, p_g))
            dve.wait_ge(pair_exp, 1)
            chain(dve.tensor_scalar(per[:, 5, 0, :], per[:, 0, 0, :], 1.0, None, ALU.add))
            chain(dve.reciprocal(per[:, 5, 0, :], per[:, 5, 0, :]))
            chain(dve.tensor_tensor(per[:, 6, 0, :], p_g, per[:, 5, 0, :], ALU.mult))
            chain(dve.tensor_tensor(per[:, 6, 1, :], per[:, 6, 0, :], per[:, 0, 0, :], ALU.mult))
            dve.wait_ge(counts_done, 1)
            chain(dve.tensor_copy(cc[:, :, :], TR[:, 0:(T + 1) * NEXP].rearrange("p (t e) -> p t e", e=NEXP)))
            over = over_cmp[:, :, :]
            chain(dve.tensor_tensor(over, spread(cc[:, T, :], [P, NEXP, 7], 2), spread(const("limit"), [P, NEXP, 7], 1),
                                    ALU.is_gt))
            chain(dve.tensor_reduce(ov[:, 0, :], over, AXX, ALU.add))
            chain(dve.tensor_tensor_scan(ov[:, 1, :], ones[:, 0:NEXP], ov[:, 0, :], 0.0, ALU.mult, ALU.add))
            chain(dve.tensor_tensor(ov[:, 2, :], ov[:, 1, :], ov[:, 0, :], ALU.subtract))
            oh8 = oh[:, :, :, :].rearrange("p k t e -> p (k t) e")
            flat = lambda q: per[:, q, :, :].rearrange("p k t -> p (k t)")
            rank, expert_of, over_of, beyond = (flat(q) for q in (7, 8, 9, 10))
            for k in range(2):
                chain(dve.tensor_tensor(tmp[:, k * T:(k + 1) * T, :], cc[:, 0:T, :], oh[:, k], ALU.mult))
            chain(dve.tensor_reduce(rank, tmp[:, :, :], AXX, ALU.add))
            chain(dve.tensor_tensor(tmp[:, :, :], oh8, spread(const("iota32"), [P, 8, NEXP], 1), ALU.mult))
            chain(dve.tensor_reduce(expert_of, tmp[:, :, :], AXX, ALU.add))
            chain(dve.tensor_tensor(tmp[:, :, :], oh8, spread(ov[:, 2, :], [P, 8, NEXP], 1), ALU.mult))
            chain(dve.tensor_reduce(over_of, tmp[:, :, :], AXX, ALU.add))
            past = over_cmp[:, 0:8, :]
            chain(dve.tensor_tensor(past, spread(rank, [P, 8, 7], 2), spread(const("limit"), [P, 8, 7], 1), ALU.is_ge))
            chain(dve.tensor_reduce(beyond, past, AXX, ALU.add))
            chain(dve.scalar_tensor_tensor(rank, beyond, -float(BLK), rank, ALU.mult, ALU.add))
            chain(dve.tensor_tensor(over_of, over_of, beyond, ALU.add))
            chain(dve.scalar_tensor_tensor(over_of, over_of, NEXP - 1.0, expert_of, ALU.add, ALU.subtract))
            chain(dve.tensor_scalar(beyond, beyond, 1.0, None, ALU.min))
            chain(dve.tensor_tensor(over_of, over_of, beyond, ALU.mult))
            chain(dve.tensor_tensor(over_of, over_of, expert_of, ALU.add))
            chain(dve.scalar_tensor_tensor(rank, rank, float(NBLK), over_of, ALU.mult, ALU.add))
            dve.tensor_copy(where[:, :], rank)
            dve.tensor_copy(info[:, :, 0], const("token"))
            dve.tensor_copy(info[:, :, 1], const("row"))
            dve.memset(info[:, :, 3], 0)
            dve.tensor_copy(info[:, :, 2].bitcast(F32), flat(6)).then_inc(routed, 1)
            over1 = over_ids[:, :, :]
            chain(dve.tensor_tensor(over1, ov[0:1, 1, :].unsqueeze(1).to_broadcast([1, MAX_OVER, NEXP]),
                                    const("iota15", 1).unsqueeze(2).to_broadcast([1, MAX_OVER, NEXP]), ALU.is_le))
            chain(dve.tensor_reduce(ctlf[:, 1:1 + MAX_OVER], over1, AXX, ALU.add))
            chain(dve.tensor_scalar(ctlf[:, 1:1 + MAX_OVER], ctlf[:, 1:1 + MAX_OVER], NEXP - 1.0, None, ALU.min))
            chain(dve.tensor_copy(ctlf[:, 0:1], ov[0:1, 1, NEXP - 1:NEXP]))
            dve.tensor_copy(ctl[:, :], ctlf[:, :]).then_inc(routed, 1)

            def turned_block(n, b2):
                dve.wait_ge(rows_turned, n + 1)
                dve.tensor_tensor(xT[b2], TR[:, :].rearrange("p (k s) -> p k s", k=KD),
                                  chn[:, G_FFN:G_FFN + KD].unsqueeze(2).to_broadcast([P, KD, BLK]),
                                  ALU.mult).then_inc(xT_ready, 1)

            def swiglu(n):
                gate = MM[:, 0:2 * BLK].rearrange("p (j s) -> p j s", j=2)
                upp = MM[:, 2 * BLK:4 * BLK].rearrange("p (j s) -> p j s", j=2)
                dve.wait_ge(gate_sig, n + 1)
                dve.tensor_tensor(sgx, gate, sgx, ALU.mult).then_inc(gate_mul, 1)
                dve.wait_ge(gate_mul, n + 1)
                dve.tensor_tensor(hx, upp, sgx, ALU.mult).then_inc(hx_ready, 1)

            def high_half(n, b2, col, buffer_free):
                dve.wait_ge(down_done, 2 * n + 2)
                buffer_free()
                dve.tensor_scalar(yr[b2][:, 512:1024], S_16[0:BLK, :], table_w(col), None, ALU.mult).then_inc(y_high, 1)

            dve.wait_ge(table_loaded, 16)
            turned_block(0, 0)
            with dve.Fori(0, NEXP // RING) as i:
                for b in range(RING):
                    n = RING * i + b
                    swiglu(n)
                    turned_block(n + 1, (b + 1) % 2)
                    high_half(n, b % 2, n, lambda b=b: dve.wait_ge(rows_scattered[b % 2], (2 * i + b // 2) * 16))
            for b in range(2):
                dve.wait_ge(rows_scattered[b], NEXP // 2 * 16)
            dve.wait_ge(routed, 2)
            n_over = dve.value_load(ctl[0:1, 0:1], min_val=0, max_val=MAX_OVER)
            with dve.Fori(0, MAX_OVER) as j:
                with dve.If(j < n_over):
                    turned_block(NEXP + 1 + j, 1)
                    swiglu(NEXP + j)
                    high_half(NEXP + j, 0, NEXP + j, lambda: dve.wait_ge(ov_scattered, j * 16))

            def x3(t):
                dve.wait_ge(rows_loaded[t % 2], (t // 2 + 1) * 32)
                chain(dve.tensor_tensor(x_sb[:, t, :], x_sb[:, t, :], yk[:, t % 2, 0, :], ALU.add))
                dve.tensor_tensor(x_sb[:, t, :], x_sb[:, t, :], yk[:, t % 2, 1, :], ALU.add).then_inc(x3_ready, 1)
                rstd(rr3[:, t:t + 1], ss3[:, t:t + 1])
                dve.tensor_scalar(n3[:, t, :], x_sb[:, t, :], rr3[:, t:t + 1], None, ALU.mult).then_inc(n3_ready, 1)

            x3(0)
            h_out(0, (S_16, OUT), n3_turned, G_PLE, h3_ready)
            for t in range(T):
                if t + 1 < T:
                    x3(t + 1)
                    h_out(t + 1, (S_16, OUT), n3_turned, G_PLE, h3_ready)
                for half in range(2):
                    cols = slice(half * 512, (half + 1) * 512)
                    dve.wait_ge(pg_sig, 2 * t + half + 1)
                    chain(dve.tensor_tensor(pple[:, t, cols], pple[:, t, cols], sg6[:, cols], ALU.mult))
                dve.tensor_tensor(x_sb[:, t, :], x_sb[:, t, :], pple[:, t, :], ALU.add).then_inc(x4_ready, 1)
                rstd(rr4[:, t:t + 1], ss4[:, t:t + 1])
                if t == 0:
                    dve.wait_ge(pg_loaded, 48)
                dve.scalar_tensor_tensor(x_sb[:, t, :], x_sb[:, t, :], rr4[:, t:t + 1], gfin_sb, ALU.mult, ALU.mult)\
                   .then_inc(out_ready, 1)

        @block.gpsimd
        def _(pool):
            pool.memset(table[:, :, :], OUT_OF_RANGE).then_inc(ready, 1)
            pool.wait_ge(ready, 1)
            pool.dma_start(table_dram.rearrange("(j b) w -> j b w", b=NBLK), table[:, :, :]).then_inc(table_blank, 16)
            pool.wait_ge(params_loaded, N_PARAMS * 16)
            pool.wait_ge(mb_ready, 5)
            with pool.Fori(0, ROUNDS) as r:
                pool.wait_ge(sgo_ready, r)
                pool.tensor_copy(slope_now[:, :], cst[:, bass.ds(_C["slope"][0] + 6 * r, 6)]).then_inc(slope_ready, 1)
                pool.wait_ge(slope_ready, r + 1)
                pool.tensor_tensor(takes_wait[:, 3:4], ones[0:1, 0:1], ones[0:1, 0:1], ALU.add)
                for s in range(2):
                    for g, (name, at, n) in enumerate((("dist1", 1024, 256), ("dist4", 0, 512), ("dist16", 512, 512))):
                        pool.tensor_scalar(bias[:, s, at:at + n], const(name),
                                           slope_now[:, 3 * s + g:3 * s + g + 1], None,
                                           ALU.mult).then_inc(bias_ready, 1)
                pool.wait_ge(qk_ready, 2 * (r + 1))
                pool.tensor_tensor(mbd.rearrange("p (t s) -> p t s", t=T),
                                   mb[:, bass.ds(r, 1), :].rearrange("p a (t s) -> p (a t) s", t=T),
                                   const("causal").unsqueeze(1).to_broadcast([P, T, P]), ALU.add).then_inc(mbd_ready, 1)
                for u in range(8):
                    i = u % 4
                    n, near = (i + 1) * P, min(i + 1, 2) * P
                    dst = psm[:, u % 2, :]
                    pool.wait_ge(exps_done, r * 8 + u + 1)
                    if u >= 2:
                        pool.wait_ge(probs_turned, r * 8 + u - 1)
                    pool.tensor_tensor(dst[:, 0:n], sc[:, u % 2, 0:n], sc[:, u % 2, n:2 * n], ALU.add).then_inc(pool_step, 1)
                    pool.wait_ge(pool_step, r * 8 + u + 1)
                    pool.tensor_tensor(dst[:, n - near:n], dst[:, n - near:n], sc[:, u % 2, 2 * n:2 * n + near],
                                       ALU.add).then_inc(probs_ready, 1)

            pool.wait_ge(merged, KD)
            pool.wait_ge(x2_mm, 2 * T)
            pool.memset(mflat[0:BLK, 0:2 * D], 0.0).then_inc(ready, 1)
            pool.wait_ge(table_blank, 16)
            pool.wait_ge(routed, 1)
            for a in range(2 * T):
                pool.indirect_dma_start(out=table_dram, out_offset=bass.IndirectOffsetOnAxis(ap=where[:, a:a + 1], axis=0),
                                        in_=info[:, a, :], in_offset=None, bounds_check=BLK * NBLK - 1,
                                        oob_is_err=False).then_inc(table_written, 16)
            pool.wait_ge(table_loaded, 16)
            pool.wait_ge(n2_stored, T * 16)
            pool.wait_ge(ready, 2)

            def take_wait(cell):
                pool.tensor_tensor(takes_wait[:, cell:cell + 1], ones[0:1, 0:1], ones[0:1, 0:1], ALU.add)

            def gather(b2, col, done, count):
                take_wait(0)
                pool.tensor_copy(gidx[:, b2:b2 + 1, :], table[:, bass.ds(col, 1), 0:2]).then_inc(idx_copied, 1)
                pool.wait_ge(idx_copied, count + 1)
                take_wait(1)
                pool.indirect_dma_start(out=xr[b2], out_offset=None, in_=normed,
                                        in_offset=bass.IndirectOffsetOnAxis(ap=gidx[:, b2, 0:1], axis=0),
                                        bounds_check=SEQ - 1, oob_is_err=False).then_inc(done, 16)

            def scatter(b2, col, done, count):
                take_wait(0)
                pool.tensor_copy(sidx[:, b2:b2 + 1, :], table[:, bass.ds(col, 1), 0:2]).then_inc(idx_copied, 1)
                pool.wait_ge(idx_copied, count + 1)
                take_wait(1)
                pool.indirect_dma_start(out=expert_rows,
                                        out_offset=bass.IndirectOffsetOnAxis(ap=sidx[:, b2, 1:2], axis=0),
                                        in_=yr[b2], in_offset=None, bounds_check=2 * SEQ - 1,
                                        oob_is_err=False).then_inc(done, 16)

            gather(0, 0, rows_gathered[0], 0)
            gather(1, 1, rows_gathered[1], 1)
            with pool.Fori(0, NEXP // RING) as i:
                for b in range(RING):
                    n = RING * i + b
                    pool.wait_ge(rows_turned, n + 1)
                    pool.wait_ge(rows_gathered[b % 2], (2 * i + b // 2 + 1) * 16)
                    gather(b % 2, n + 2, rows_gathered[b % 2], 2 + 2 * n)
                    pool.wait_ge(y_low, n + 1)
                    pool.wait_ge(y_high, n + 1)
                    pool.wait_ge(rows_scattered[b % 2], (2 * i + b // 2) * 16)
                    scatter(b % 2, n, rows_scattered[b % 2], 3 + 2 * n)
            for b in range(2):
                pool.wait_ge(rows_gathered[b], (NEXP // 2 + 1) * 16)
                pool.wait_ge(rows_scattered[b], NEXP // 2 * 16)
            pool.wait_ge(rows_turned, NEXP + 1)
            pool.wait_ge(routed, 2)
            n_over = pool.value_load(ctl[0:1, 0:1], min_val=0, max_val=MAX_OVER)
            with pool.Fori(0, MAX_OVER) as j:
                with pool.If(j < n_over):
                    pool.wait_ge(rows_turned, NEXP + 1 + j)
                    gather(0, NEXP + j, ov_gathered, 2 + 2 * NEXP + 2 * j)
                    pool.wait_ge(y_low, NEXP + 1 + j)
                    pool.wait_ge(y_high, NEXP + 1 + j)
                    scatter(0, NEXP + j, ov_scattered, 3 + 2 * NEXP + 2 * j)
                    pool.wait_ge(ov_scattered, (j + 1) * 16)
            pool.memset(small[:, 95:96], 0.0).then_inc(ov_all, 1)


def layout(a):
    f = lambda n: a[n][0]
    c = np.ascontiguousarray

    def tiles(w):
        return w.reshape(-1, P, w.shape[-1]).transpose(1, 0, 2)

    w = tiles(f("w_in"))
    cols = lambda at, n=P: w[:, :, at:at + n]
    cm = [[cols(at + r * P) for at in (CONV0 + CH, CONV0, MQ0, MK0, Q0, Q0 + 512, Q0 + 1024, K0)] for r in range(ROUNDS)]
    tm = [np.concatenate([cols(V0 + r * P), cols(MO0 + r * P), cols(MV0 + r * P)], -1) for r in range(ROUNDS)]
    order = ((0, "w_br_att"), (2, "w_br_mlstm"), (1, "w_br_conv"))
    gate = [[cols(GATE0 + b * D + dt * P) for b, _ in order] for dt in range(KD)]
    branch = [[tiles(f(n))[:, :, dt * P:(dt + 1) * P] for _, n in order] for dt in range(KD)]
    per = lambda v: v.reshape(-1, P).T
    mw, mb_ = f("mlstm_conv_w"), f("mlstm_conv_b")
    chan = [per(f("g_mix")), per(f("g_ffn")), per(f("g_ple"))]
    chan += [f("conv_w")[:, r * P:(r + 1) * P].T for r in range(ROUNDS)]
    chan += [per(f("conv_b")), per(f("conv_ln_g")), per(f("conv_ln_b"))]
    for r in range(ROUNDS):
        q, k = slice(r * P, (r + 1) * P), slice(CH + r * P, CH + (r + 1) * P)
        chan += [mw[:, q].T, mw[:, k].T, mb_[q][:, None], mb_[k][:, None]]
    chan += [np.full((P, 1), EPS, np.float32)]
    chan = np.concatenate(chan, 1)
    assert chan.shape == (P, NCHAN)
    experts = np.concatenate([
        np.concatenate([f("w_exp_gate"), f("w_exp_up")], -1).reshape(NEXP, KD, P, 2 * HID).transpose(0, 2, 1, 3)
        .reshape(NEXP, P, -1),
        f("w_exp_down").reshape(NEXP, 2, P, D).transpose(0, 2, 1, 3).reshape(NEXP, P, -1)], -1)
    return {k: c(v) for k, v in {
        "x": a["x"][0],
        "consts": constants(),
        "chan": chan,
        "if_bias": np.concatenate([f("mlstm_i_bias"), f("mlstm_f_bias")]),
        "r_bias": np.concatenate([f("b_router_g"), f("b_router_e")]),
        "g_final": a["g_final"],
        "w_cm": np.stack([np.stack(x) for x in cm]).reshape(ROUNDS, 8, P, KD * P),
        "w_tm": np.stack(tm),
        "w_if": cols(IF0, 8).reshape(P, -1),
        "w_gate": np.stack([np.stack(x, 1) for x in gate]).reshape(KD, P, 3, KD * P),
        "w_branch": np.stack([np.stack(x, 1) for x in branch]).reshape(KD, P, 3, 4 * P),
        "w_out": tiles(f("w_out")),
        "w_router": tiles(np.concatenate([f("w_router_g"), f("w_router_e")], -1)),
        "w_expert": experts,
        "w_pg": tiles(f("w_ple_gate")).reshape(P, 2, -1).transpose(1, 0, 2),
        "w_pp": tiles(f("w_ple_proj")),
        "pT": tiles(f("p")[0].T),
    }.items()}


def kernel(**inputs):
    import numpy as _np
    import concourse.bacc as _bacc
    from concourse import mybir as _mybir
    from concourse.bass_utils import run_bass_kernel_spmd as _run

    a = {k: _np.asarray(v) for k, v in inputs.items()}
    arrays = layout(a)
    nc = _bacc.Bacc("TRN2", target_bir_lowering=False, num_devices=1)
    args = [nc.dram_tensor(f"in_{n}", v.shape, _mybir.dt.from_np(v.dtype), kind="ExternalInput").ap()
            for n, v in arrays.items()]
    args.append(nc.dram_tensor("out_0", (SEQ, D), F32, kind="ExternalOutput").ap())
    build(nc, *args)
    r = _run(nc, [{f"in_{n}": v for n, v in arrays.items()}], core_ids=[0])
    return r.results[0]["out_0"].reshape(1, SEQ, D)
```

```python
from contextlib import ExitStack

import numpy as np

import concourse.bass as bass
from concourse import mybir

F32 = mybir.dt.float32
F32R = mybir.dt.float32r
I32 = mybir.dt.int32
ALU = mybir.AluOpType
ACT = mybir.ActivationFunctionType
AXX = mybir.AxisListType.X

P = 128
D = 1024
SEQ = 512
T = SEQ // P
KD = D // P
HEAD = 64
SLOTS = 8
DILATIONS = (1, 4, 16)
STEPS = 128
ROUNDS = 4
CH = 512
CONV_K = 31
MCONV_K = 4
DH = 128
NGROUP, PER_GROUP = 4, 8
NEXP = NGROUP * PER_GROUP
HID = 256
PLE = 256
EPS = 1e-6
BLK = 64
M_AT = (0, 4 * P, 7 * P, 9 * P)
CM_CREDIT = 4
FREE = 1
CONV_STEPS = CONV_K + 2 * MCONV_K
MAX_OVER = (2 * SEQ - NEXP) // BLK
NBLK = 48
OUT_OF_RANGE = 4096
BIG = 1e30
RING = 4
Q0, K0, V0, CONV0, MQ0, MK0, MV0, MO0, IF0, GATE0 = (
    0, 1536, 2048, 2560, 3584, 4096, 4608, 5120, 5632, 5640)

_C = {}
_at = 0
for _name, _n in (("ident", P), ("upper", P), ("ones", P), ("mean", P), ("causal", P),
                  ("dist4", SEQ), ("dist16", SEQ), ("dist1", 2 * P), ("sel", 4 * P), ("rev32", NEXP),
                  ("iota32", NEXP), ("rev4", NGROUP), ("limit", 7), ("iota15", MAX_OVER),
                  ("slope", 3 * SLOTS), ("token", 2 * T), ("row", 2 * T)):
    _C[_name] = (_at, _n)
    _at += _n
NCONST = _at
G_MIX, G_FFN, G_PLE, CONV_W, CONV_B, LN_G, LN_B, MCONV, EPS_COL, NCHAN = (
    0, 8, 16, 24, 148, 152, 156, 160, 200, 201)


def constants():
    c = np.zeros((P, NCONST), np.float32)

    def put(name, value):
        at, n = _C[name]
        c[:, at:at + n] = value

    row, col = np.arange(P)[:, None], np.arange(P)[None, :]
    put("ident", row == col)
    put("upper", row < col)
    put("ones", 1.0)
    put("mean", 1.0 / CH)
    put("causal", np.where(row > col, BIG, 0.0))
    for name, dil, blocks in (("dist1", 1, 2), ("dist4", 4, 4), ("dist16", 16, 4)):
        d = row + (blocks - 1) * P - np.arange(blocks * P)[None, :]
        ok = (d >= 0) & (d % dil == 0) & (d <= dil * STEPS)
        put(name, np.where(ok, -d, -BIG))
    sel = np.zeros((P, 4, P))
    for h in range(4):
        sel[h, h] = 1.0
    put("sel", sel.reshape(P, 4 * P))
    put("rev32", NEXP - np.arange(NEXP)[None])
    put("iota32", np.arange(NEXP)[None])
    put("rev4", NGROUP - np.arange(NGROUP)[None])
    put("limit", BLK * np.arange(1, 8)[None])
    put("iota15", np.arange(MAX_OVER)[None])
    j = np.arange(1, 3 * SLOTS + 1, dtype=np.float32)
    slopes = (np.float32(2.0) ** (-np.float32(8.0) * j / np.float32(24))).reshape(3, SLOTS // 2, 2)
    put("slope", slopes.transpose(1, 2, 0).reshape(1, -1))
    k, t = np.divmod(np.arange(2 * T), T)
    put("token", t[None] * P + row)
    put("row", k[None] * SEQ + t[None] * P + row)
    return c


def build(nc, x, consts, chan, if_bias, r_bias, g_final, w_cm, w_tm, w_if, w_gate, w_branch, w_out,
          w_router, w_expert, w_pg, w_pp, pT, out):
    normed = nc.dram_tensor("normed", [SEQ, D], F32, kind="Internal").ap()
    expert_rows = nc.dram_tensor("expert_rows", [2 * SEQ, D], F32, kind="Internal").ap()
    table_dram = nc.dram_tensor("table_dram", [BLK * NBLK, 4], I32, kind="Internal").ap()

    with ExitStack() as ctx:
        offset_of = {}

        def sb(name, shape, dt=F32):
            offset_of[name] = -(-nc.sbuf_base // 32) * 32
            return ctx.enter_context(nc.sbuf_tensor(name, shape, dt))

        def sem(name):
            return ctx.enter_context(nc.semaphore(name))

        x_sb = sb("x_sb", [P, T, D])
        hT = sb("hT", [P, KD, SEQ])
        mT = sb("mT", [P, KD, SEQ])
        cst = sb("cst", [P, NCONST])
        chn = sb("chn", [P, NCHAN])
        yT = sb("yT", [P, 3, ROUNDS, SEQ])
        arena = sb("arena", [P, 116 * 256])

        def parts_in(name, tensor, shape, skip=0):
            return nc.alloc_sbuf_tensor_at(name, shape, F32R, offset=offset_of[tensor] + 4 * skip)

        x_parts = parts_in("x_parts", "x_sb", [P, T * D])
        hT_parts = parts_in("hT_parts", "hT", [P, KD, SEQ])
        mT_parts = parts_in("mT_parts", "mT", [P, KD, SEQ])
        low_parts = parts_in("low_parts", "arena", [P, 30 * 256], 48 * 256)
        if_b = sb("if_b", [P, 8])
        r_b = sb("r_b", [P, 36])
        small = sb("small", [P, 96])
        banks = [ctx.enter_context(nc.psum_tensor(f"bank{i}", [P, 512], F32)) for i in range(8)]
        PA, PB, S_1, S_4, S_16, TR, OUT, MM = banks

        def const(name, rows=P):
            at, n = _C[name]
            return cst[0:rows, at:at + n]

        ident, ones = const("ident"), const("ones")

        class Place:

            def __init__(self, kib, memory=arena):
                self.at = int(kib * 256)
                self.memory = memory

            def take(self, *shape):
                n = int(np.prod(shape))
                piece = self.memory[:, self.at:self.at + n]
                self.at += n
                assert self.at <= 116 * 256
                names = "abc"[:len(shape)]
                if len(shape) > 1:
                    piece = piece.rearrange(f"p ({' '.join(names)}) -> p {' '.join(names)}",
                                            **dict(zip(names, shape)))
                return piece

        pl = Place(0)
        bias = pl.take(2, 1280)
        bias_flat = arena[:, 0:2560]
        sc = pl.take(2, 1280)
        psm = pl.take(2, SEQ)
        pT_sb = pl.take(2, SEQ)
        oatt = pl.take(T, P)
        ypad = pl.take(CONV_K - 1 + SEQ)
        cacc = pl.take(2, SEQ)
        sgt = pl.take(SEQ)
        qT = pl.take(3, SEQ)
        kT = pl.take(SEQ)
        gone = pl.at
        wcm = Place(48).take(4, KD * P)
        wtm = Place(64).take(KD, 3 * P)
        assert gone <= 48 * 256, gone
        pl = Place(76)
        tmv = pl.take(T, 3 * P + 1)
        raw = pl.take(2, MCONV_K - 1 + SEQ)
        qk = pl.take(2, SEQ)
        sqk = pl.take(2, SEQ)
        mb = pl.take(4, SEQ)
        mbd = sqk[:, 0, :]
        wm = pl.take(1280)
        wms = wm
        ym = pl.take(T, P)
        assert pl.at + KD * P <= 116 * 256
        cm_high_b = parts_in("cm_high_b", "arena", [P, KD * P], -(-pl.at // 8) * 8)[:, :]
        sgo = sgt.rearrange("p (t c) -> p t c", t=T)
        rows = Place(20).take(5, SEQ)
        wg = [Place(48).take(3, KD * P), Place(66).take(3, KD * P)]
        wb = [Place(60).take(3, 4 * P), Place(78).take(3, 4 * P)]
        wo = Place(84).take(KD, D)
        pl = Place(84)
        lnt = pl.take(ROUNDS, SEQ)
        sgl = pl.take(ROUNDS, SEQ)
        rst = pl.take(SEQ)
        lnr = pl.take(SEQ)
        pl = Place(24)
        sgm = pl.take(3, SEQ)
        mp = pl.take(3, SEQ)
        merged_T = Place(0).take(KD, SEQ)
        we = [Place(24 * b).take(6144) for b in range(RING)]
        yflat = yT[:, :, :, :].rearrange("p b r s -> p (b r s)")
        n2 = yflat[:, 0:T * D].rearrange("p (t d) -> p t d", t=T)
        pple = n2
        xT = [yflat[:, 4096 + b * 512:4608 + b * 512].rearrange("p (k s) -> p k s", k=KD) for b in range(2)]
        h_high, h_low = mT_parts, hT_parts
        wtm_high = x_parts[:, 0:3 * D].rearrange("p (k c) -> p k c", k=KD)
        cm_high = [x_parts[:, 3 * D:4 * D], cm_high_b]
        gate_high = [x_parts[:, br * D:(br + 1) * D] for br in range(3)]
        wcm_low = Place(0, low_parts).take(4, KD * P)
        wtm_low = Place(16, low_parts).take(KD, 3 * P)
        wg_low = [Place(at, low_parts).take(3, KD * P) for at in (0, 18)]
        hx = yflat[:, 5120:5248].rearrange("p (j s) -> p j s", j=2)
        sgx = yflat[:, 5248:5376].rearrange("p (j s) -> p j s", j=2)
        pl = Place(96)
        p_in = pl.take(2, SEQ)
        pple_w = pl.take(2, D)
        junk1, junk2, junk3 = bias_flat[:, 0:D], Place(78).take(D), Place(72).take(D)
        sg6 = Place(76).take(2, D)
        pl = Place(96)
        yk01, yk23 = pl.take(2, 2, D), Place(48).take(2, 2, D)
        yk = [yk01[:, 0], yk01[:, 1], yk23[:, 0], yk23[:, 1]]
        gfin_sb = pl.take(D)
        mT_tok = mT[:, :, :].rearrange("p k s -> p (k s)").rearrange("p (t d) -> p t d", t=T)
        mflat = mT[:, :, :].rearrange("p k s -> p (k s)")
        xr = [mflat[0:BLK, b * D:(b + 1) * D] for b in range(2)]
        yr = [mflat[0:BLK, (2 + b) * D:(3 + b) * D] for b in range(2)]
        wr_sb = sb("wr_sb", [P, KD, 36])
        rl = sb("rl", [P, T, 36])
        le = sb("le", [P, T, NEXP])
        oh = sb("oh", [P, 2, T, NEXP])
        tmp = sb("tmp", [P, 8, NEXP])
        oh4 = sb("oh4", [P, T, NGROUP])
        t4 = sb("t4", [P, T, NGROUP])
        cc = sb("cc", [P, T + 1, NEXP])
        ov = sb("ov", [P, 3, NEXP])
        per = sb("per", [P, 12, 2, T])
        info = sb("info", [P, 2 * T, 4], I32)
        where = sb("where", [P, 2 * T], I32)
        ctl = sb("ctl", [1, 16], I32)
        ctlf = sb("ctlf", [1, 16])
        table = sb("table", [BLK, NBLK, 4], I32)
        gidx = sb("gidx", [BLK, 2, 2], I32)
        sidx = sb("sidx", [BLK, 2, 2], I32)
        over_cmp = mflat[:, 3072:3296].rearrange("p (e m) -> p e m", m=7)
        over_ids = mflat[0:1, 2048:2048 + MAX_OVER * NEXP].rearrange("p (b e) -> p b e", e=NEXP)

        def table_w(col):
            return table[:, bass.ds(col, 1), 2:3].rearrange("p a b -> p (a b)").bitcast(F32)

        ss, rr, ss2, rr2, ss3, rr3, ss4, rr4 = (small[:, 4 * i:4 * i + 4] for i in range(8))
        mx3 = small[:, 32:38].rearrange("p (b g) -> p b g", b=2)
        nmx = small[:, 38:40]
        den = small[:, 40:48]
        rden = small[:, 48:56]
        ucol = sb("ucol", [P, T, 4])
        ecol = sb("ecol", [P, T, 4])
        slope_now = sb("slope_now", [P, 6])
        md = sb("md", [P, 2, T])
        ifs = sb("ifs", [P, T, 8])
        lft = sb("lft", [P, 3, T, 4])

        x_loaded = [sem(f"x_loaded{t}") for t in range(T)]
        chan_loaded = sem("chan_loaded")
        ident_loaded = sem("ident_loaded")
        consts_loaded = sem("consts_loaded")
        w_if_loaded = sem("w_if_loaded")
        params_loaded = sem("params_loaded")
        cell_set = sem("cell_set")
        ready = sem("ready")
        x_squared = sem("x_squared")
        rooted = sem("rooted")
        ln_root = sem("ln_root")
        dve_step = sem("dve_step")
        act_step = sem("act_step")
        x_normed = sem("x_normed")
        x_turned = sem("x_turned")
        h_ready = sem("h_ready")
        if_projected = sem("if_projected")
        if_ready = sem("if_ready")
        lf_ready = sem("lf_ready")
        if_turned = sem("if_turned")
        prefix_ready = sem("prefix_ready")
        em_ready = sem("em_ready")
        max_spread = sem("max_spread")
        cols_turned = sem("cols_turned")
        mb_ready = sem("mb_ready")
        cm_loaded = [sem(f"cm_loaded{s}") for s in range(4)]
        cm_done = sem("cm_done")
        rounded = sem("rounded")
        h_rounded = sem("h_rounded")
        h_split = [sem("h_split_dve"), sem("h_split_pool")]
        cm_split = sem("cm_split")
        tm_split = sem("tm_split")
        gate_split = sem("gate_split")
        tm_loaded = sem("tm_loaded")
        tm_done = sem("tm_done")
        bank_read = [sem("bank_a_read"), sem("bank_b_read")]
        conv_step = sem("conv_step")
        conv_ready = sem("conv_ready")
        mq_sig = sem("mq_sig")
        qk_ready = sem("qk_ready")
        slope_ready = sem("slope_ready")
        bias_ready = sem("bias_ready")
        mbd_ready = sem("mbd_ready")
        scores_done = sem("scores_done")
        biased = sem("biased")
        negmax_ready = sem("negmax_ready")
        exps_done = sem("exps_done")
        pool_step = sem("pool_step")
        probs_ready = sem("probs_ready")
        probs_turned = sem("probs_turned")
        pt_ready = sem("pt_ready")
        pv_done = sem("pv_done")
        rden_ready = sem("rden_ready")
        att_out = sem("att_out")
        att_turned = sem("att_turned")
        m_scores = sem("m_scores")
        m_weights = sem("m_weights")
        m_weighted = sem("m_weighted")
        m_num = sem("m_num")
        sgo_ready = sem("sgo_ready")
        md_step = sem("md_step")
        ym_ready = sem("ym_ready")
        ym_turned = sem("ym_turned")
        y_ready = sem("y_ready")
        ln_mm = sem("ln_mm")
        ln_step = sem("ln_step")
        ln_act = sem("ln_act")
        yconv_ready = sem("yconv_ready")
        mw_loaded = [sem("mw_loaded0"), sem("mw_loaded1")]
        gate_done = sem("gate_done")
        branch_done = sem("branch_done")
        gate_read = sem("gate_read")
        branch_read = sem("branch_read")
        merge_step = sem("merge_step")
        merged = sem("merged")
        wo_loaded = sem("wo_loaded")
        x2_mm = sem("x2_mm")
        x2_ready = sem("x2_ready")
        x2_squared = sem("x2_squared")
        n2_ready = sem("n2_ready")
        n2_stored = sem("n2_stored")
        x2_turned = sem("x2_turned")
        h2_ready = sem("h2_ready")
        logits_done = sem("logits_done")
        group_exp = sem("group_exp")
        pair_exp = sem("pair_exp")
        shifted = sem("shifted")
        diff_ready = sem("diff_ready")
        onehots = sem("onehots")
        counts_done = sem("counts_done")
        routed = sem("routed")
        table_written = sem("table_written")
        table_loaded = sem("table_loaded")
        pw_loaded = sem("pw_loaded")
        ple_mm = sem("ple_mm")
        ple_copied = sem("ple_copied")
        we_loaded = [sem(f"we_loaded{b}") for b in range(RING)]
        idx_copied = sem("idx_copied")
        rows_gathered = [sem("rows_gathered0"), sem("rows_gathered1")]
        rows_turned = sem("rows_turned")
        xT_ready = sem("xT_ready")
        g_done = sem("g_done")
        u_done = sem("u_done")
        gate_sig = sem("gate_sig")
        gate_mul = sem("gate_mul")
        hx_ready = sem("hx_ready")
        down_done = sem("down_done")
        y_low = sem("y_low")
        y_high = sem("y_high")
        rows_scattered = [sem("rows_scattered0"), sem("rows_scattered1")]
        ov_w = sem("ov_w")
        ov_gathered = sem("ov_gathered")
        ov_all = sem("ov_all")
        rows_loaded = [sem(f"rows_loaded{t}") for t in range(T)]
        pg_loaded = sem("pg_loaded")
        x3_ready = sem("x3_ready")
        x3_squared = sem("x3_squared")
        x3_rstd = sem("x3_rstd")
        x3_turned = sem("x3_turned")
        h3_ready = sem("h3_ready")
        pg_mm = sem("pg_mm")
        pg_sig = sem("pg_sig")
        x4_ready = sem("x4_ready")
        x4_squared = sem("x4_squared")
        out_ready = sem("out_ready")
        stored = sem("stored")

        N_PARAMS = 3
        H_DVE = 5
        CM_TILES_AT = {8: 4, 14: 5, 22: 6, 28: 7}
        TM_AFTER, TM_TILE_AT = 4, 10
        SCATTERED = (1 + NEXP // 2) * 16

        CM_ORDER = 8
        takes_wait = sb("takes_wait", [1, 4])

        block = ctx.enter_context(nc.Block())

        @block.sync
        def _(sp):
            sp.dma_start(chn[:, :], chan).then_inc(chan_loaded, 16)
            for t in range(T):
                sp.dma_start(x_sb[:, t, :], x[t * P:(t + 1) * P, :]).then_inc(x_loaded[t], 16)
                if t == 0:
                    sp.dma_start(cst[:, 0:P], consts[:, 0:P]).then_inc(ident_loaded, 16)
                    sp.dma_start(wtm[:, 0, 0:KD * 8], w_if).then_inc(w_if_loaded, 16)
            sp.dma_start(cst[:, P:], consts[:, P:]).then_inc(consts_loaded, 16)
            for dst, src in ((if_b[:, :], if_bias.partition_broadcast(P)),
                             (r_b[:, :], r_bias.partition_broadcast(P)),
                             (wr_sb[:, :, :], w_router)):
                sp.dma_start(dst, src).then_inc(params_loaded, 16)

            with sp.Fori(0, ROUNDS) as r:
                for n in range(CM_ORDER):
                    sp.wait_ge(cm_done, r * CM_ORDER + n + 1)
                    sp.dma_start(wcm[:, n % 4, :], w_cm[r, n, :, :]).then_inc(cm_loaded[n % 4], 16)
                    if n == 4:
                        sp.wait_ge(if_projected, T)
                        sp.dma_start(wtm, w_tm[r, :, :, :]).then_inc(tm_loaded, 16)

            def merge_weights(slot, dt):
                sp.dma_start(wg[slot], w_gate[dt, :, :, :]).then_inc(mw_loaded[slot], 16)
                sp.dma_start(wb[slot], w_branch[dt, :, :, :]).then_inc(mw_loaded[slot], 16)

            sp.wait_ge(cm_done, CM_CREDIT + ROUNDS * CM_ORDER)
            sp.wait_ge(tm_done, ROUNDS * T)
            merge_weights(0, 0)
            sp.wait_ge(y_ready, FREE + 2 * ROUNDS)
            merge_weights(1, 1)

            def expert_weights(b, e):
                sp.dma_start(we[b], w_expert[e, :, :]).then_inc(we_loaded[b], 16)

            sp.wait_ge(yconv_ready, ROUNDS)
            sp.dma_start(wo, w_out).then_inc(wo_loaded, 16)

            with sp.Fori(0, KD // 2 - 1) as i:
                for s in range(2):
                    sp.wait_ge(branch_done, 3 * (2 * i + s + 1))
                    merge_weights(s, 2 * i + s + 2)
            sp.wait_ge(gate_done, 3 * KD)
            for t in range(T):
                sp.dma_start(x_sb[:, t, :], x[t * P:(t + 1) * P, :]).then_inc(x_loaded[t], 16)
            sp.wait_ge(merged, FREE + KD)
            expert_weights(1, 1)
            expert_weights(2, 2)
            for t in range(T):
                sp.wait_ge(n2_ready, t + 1)
                sp.dma_start(normed[t * P:(t + 1) * P, :], n2[:, t, :]).then_inc(n2_stored, 16)
            sp.wait_ge(x2_mm, 2 * T)
            expert_weights(0, 0)
            sp.wait_ge(x2_squared, T)
            sp.dma_start(pple_w, w_pp).then_inc(pw_loaded, 16)
            sp.dma_start(p_in, pT).then_inc(pw_loaded, 16)
            expert_weights(3, 3)
            sp.wait_ge(table_written, 2 * T * 16)
            sp.dma_start(table[:, :, :], table_dram.rearrange("(j b) w -> j b w", b=NBLK)).then_inc(table_loaded, 16)
            sp.wait_ge(routed, 2)
            n_over = sp.value_load(ctl[0:1, 0:1], min_val=0, max_val=MAX_OVER)
            with sp.Fori(0, NEXP // RING - 1) as i:
                for b in range(RING):
                    sp.wait_ge(down_done, 2 * (RING * i + b + 1))
                    expert_weights(b, RING * (i + 1) + b)
            for half in range(2):
                sp.wait_ge(down_done, 2 * (NEXP - RING + half + 1))
                sp.dma_start(we[half][:, 0:4096], w_pg[half, :, :]).then_inc(pg_loaded, 16)
            sp.wait_ge(down_done, 2 * NEXP)
            sp.dma_start(gfin_sb, g_final.partition_broadcast(P)).then_inc(pg_loaded, 16)
            with sp.If(n_over > 0):
                with sp.Fori(0, MAX_OVER) as j:
                    with sp.If(j < n_over):
                        sp.wait_ge(down_done, 2 * (NEXP + j))
                        e = sp.value_load(ctl[0:1, bass.ds(j + 1, 1)], min_val=0, max_val=NEXP - 1)
                        sp.dma_start(we[3], w_expert[e, :, :]).then_inc(ov_w, 16)

            sp.wait_ge(ov_all, 1)
            for t in range(T):
                for k in range(2):
                    sp.dma_start(yk[t][:, k, :],
                                 expert_rows[k * SEQ + t * P:k * SEQ + (t + 1) * P, :]).then_inc(rows_loaded[t], 16)
            for t in range(T):
                sp.wait_ge(out_ready, t + 1)
                sp.dma_start(out[t * P:(t + 1) * P, :], x_sb[:, t, :]).then_inc(stored, 16)
            sp.wait_ge(stored, T * 16)

        @block.scalar
        def _(act):
            roots = [0]

            def root(dst, total, squared, count):
                roots[0] += 1
                act.wait_ge(squared, count)
                act.activation(dst, total, ACT.Sqrt, scale=1.0 / D, bias=chn[:, EPS_COL:EPS_COL + 1]).then_inc(rooted, 1)

            act.wait_ge(cell_set, 1)
            act.activation(small[:, 94:95], small[:, 94:95], ACT.Sqrt).then_inc(cell_set, 1)
            act.wait_ge(chan_loaded, 16)
            for t in range(T):
                act.wait_ge(x_loaded[t], 16)
                if t:
                    act.wait_ge(x_squared, t)
                act.activation(junk1, x_sb[:, t, :], ACT.Square, accum_out=ss[:, t:t + 1]).then_inc(x_squared, 1)
                root(rr[:, t:t + 1], ss[:, t:t + 1], x_squared, t + 1)
            def round_cm(r, n):
                act.wait_ge(cm_loaded[n % 4], (2 * r + n // 4 + 1) * 16)
                act.wait_ge(cm_done, CM_CREDIT + r * CM_ORDER + n - 1)
                act.activation(cm_high[n % 2], wcm[:, n % 4, :], ACT.Copy).then_inc(rounded, 1)

            def round_gate(s, br):
                act.activation(gate_high[br], wg[s][:, br, :], ACT.Copy).then_inc(rounded, 1)

            act.wait_ge(x_normed, T)
            for n in range(2):
                round_cm(0, n)
            act.wait_ge(if_ready, 1)
            act.activation(lft[:, 0], ifs[:, :, 4:8], ACT.Abs).then_inc(act_step, 1)
            act.wait_ge(act_step, 1)
            act.activation(lft[:, 1], lft[:, 0], ACT.Exp, scale=-1.0).then_inc(act_step, 1)
            act.wait_ge(act_step, 2)
            act.activation(lft[:, 2], lft[:, 1], ACT.Ln, bias=1.0).then_inc(act_step, 1)
            act.wait_ge(prefix_ready, 5)
            act.activation(rows[0:4, 4, :], rows[0:4, 3, :], ACT.Exp, scale=-1.0).then_inc(em_ready, 1)

            def one_round(r, last=False):
                def unit(u):
                    return r * 8 + u + 1

                act.wait_ge(cm_done, CM_CREDIT + r * CM_ORDER + 1)
                act.activation(sgt, PA[:, :], ACT.Sigmoid).then_inc(bank_read[0], 1)
                round_cm(r, 2)
                round_cm(r, 3)
                for n, dst, scale in ((2, raw[:, 0, MCONV_K - 1:], 1.0), (3, raw[:, 1, MCONV_K - 1:], 1.0),
                                      (4, qT[:, 0], HEAD ** -0.5), (5, qT[:, 1], HEAD ** -0.5),
                                      (6, qT[:, 2], HEAD ** -0.5), (7, kT, 1.0)):
                    act.wait_ge(cm_done, CM_CREDIT + r * CM_ORDER + n + 1)
                    act.activation(dst, (PA, PB)[n % 2][:, :], ACT.Copy, scale=scale).then_inc(bank_read[n % 2], 1)
                    if n < 6:
                        round_cm(r, n + 2)
                    if n == TM_AFTER - 2:
                        act.wait_ge(tm_loaded, (r + 1) * 16)
                        act.activation(wtm_high, wtm, ACT.Copy).then_inc(rounded, 1)
                for c in range(2):
                    act.wait_ge(conv_step, r * CONV_STEPS + CONV_K + 4 * (c + 1))
                    act.activation(sqk[:, c], qk[:, c], ACT.Sigmoid).then_inc(mq_sig, 1)

                def pt_copy(u):
                    n = (u % 4 + 1) * P
                    act.wait_ge(probs_turned, unit(u))
                    act.activation(pT_sb[:, u % 2, 0:n], TR[:, 0:n], ACT.Copy).then_inc(pt_ready, 1)

                for u in range(8):
                    i = u % 4
                    n = min(i + 1, 2) * P + 2 * (i + 1) * P
                    act.wait_ge(negmax_ready, unit(u))
                    act.activation(sc[:, u % 2, 0:n], sc[:, u % 2, 0:n], ACT.Exp, bias=nmx[:, u % 2:u % 2 + 1],
                                   accum_out=den[:, u:u + 1]).then_inc(exps_done, 1)
                    if u < T:
                        act.wait_ge(tm_done, r * T + u + 1)
                        act.activation(tmv[:, u, 0:3 * P], (PA, PB)[u % 2][:, 0:3 * P], ACT.Copy)\
                           .then_inc(bank_read[u % 2], 1)
                    if u >= 1:
                        pt_copy(u - 1)
                    if 3 <= u < 5 and not last:
                        round_cm(r + 1, u - 3)
                    if 3 <= u < 6 and last:
                        act.wait_ge(mw_loaded[0], 32)
                        round_gate(0, u - 3)
                    if 2 <= u < 6:
                        j = u - 2
                        at, width = M_AT[j], (T - j) * P
                        act.wait_ge(mbd_ready, r + 1)
                        act.activation(wm[:, at:at + P], mbd[:, j * P:(j + 1) * P], ACT.Exp,
                                       bias=ucol[:, j, bass.ds(r, 1)], scale=-1.0).then_inc(m_weights, 1)
                        if j < T - 1:
                            act.activation(wm[:, at + P:at + width], mb[:, bass.ds(r, 1), (j + 1) * P:], ACT.Exp,
                                           bias=ucol[:, j, bass.ds(r, 1)], scale=-1.0).then_inc(m_weights, 1)
                act.activation(sgo, tmv[:, :, P:2 * P], ACT.Sigmoid).then_inc(sgo_ready, 1)
                pt_copy(7)
                act.wait_ge(att_turned, r + 1)
                act.activation(yT[:, 0, bass.ds(r, 1), :], TR[:, :], ACT.Copy).then_inc(y_ready, 1)
                act.wait_ge(ym_turned, r + 1)
                act.activation(yT[:, 1, bass.ds(r, 1), :], MM[:, :], ACT.Copy).then_inc(y_ready, 1)

            with act.Fori(0, ROUNDS - 1) as r:
                one_round(r)
            one_round(ROUNDS - 1, last=True)

            act.sem_inc(gate_read, 3)
            act.wait_ge(ln_step, 4)
            for c in range(ROUNDS):
                act.activation(lnt[:, c], yT[:, 2, c, :], ACT.Square).then_inc(ln_act, 1)
            act.wait_ge(ln_step, 5)
            act.activation(lnr, rst, ACT.Sqrt).then_inc(ln_root, 1)
            for c in range(ROUNDS):
                act.wait_ge(ln_step, 6 + c)
                act.activation(sgl[:, c], yT[:, 2, c, :], ACT.Sigmoid, scale=chn[:, LN_G + c:LN_G + c + 1],
                               bias=chn[:, LN_B + c:LN_B + c + 1]).then_inc(ln_act, 1)

            def gate_tile(h, s, last=False):
                dt = 2 * h + s
                for br in range(3):
                    act.wait_ge(gate_done, dt * 3 + br + 1)
                    act.wait_ge(merged, FREE + dt)
                    act.activation(sgm[:, br], (PA, S_1, S_16)[br][:, :], ACT.Sigmoid).then_inc(gate_read, 1)
                    if not last:
                        if br == 0:
                            act.wait_ge(mw_loaded[1 - s], (h + s + 1) * 32)
                        round_gate(1 - s, br)

            with act.Fori(0, KD // 2 - 1) as h:
                for s in range(2):
                    gate_tile(h, s)
            gate_tile(KD // 2 - 1, 0)
            gate_tile(KD // 2 - 1, 1, last=True)

            for t in range(T):
                act.wait_ge(x2_ready, 2 * (t + 1))
                if t:
                    act.wait_ge(x2_squared, t)
                act.activation(junk2, x_sb[:, t, :], ACT.Square, accum_out=ss2[:, t:t + 1]).then_inc(x2_squared, 1)
                root(rr2[:, t:t + 1], ss2[:, t:t + 1], x2_squared, t + 1)
            act.wait_ge(shifted, 1)
            act.activation(t4[:, :, :], t4[:, :, :], ACT.Exp).then_inc(group_exp, 1)
            act.wait_ge(diff_ready, 1)
            act.activation(per[:, 0, 0, :], per[:, 0, 1, :], ACT.Exp).then_inc(pair_exp, 1)
            for t in range(T):
                act.wait_ge(ple_mm, 2 * (t + 1))
                for half in range(2):
                    act.activation(pple[:, t, half * 512:(half + 1) * 512], (PA, PB, S_1, S_4)[(2 * t + half) % 4][:, :],
                                   ACT.Copy).then_inc(ple_copied, 1)

            def expert(n, b2, col, first_wait):
                act.wait_ge(g_done, n + 1)
                act.activation(sgx, MM[:, 0:2 * BLK], ACT.Sigmoid).then_inc(gate_sig, 1)
                act.wait_ge(down_done, 2 * n + 1)
                first_wait()
                act.activation(yr[b2][:, 0:512], OUT[0:BLK, :], ACT.Copy,
                               scale=table_w(col)).then_inc(y_low, 1)

            act.wait_ge(table_loaded, 16)
            act.wait_ge(routed, 2)
            n_over = act.value_load(ctl[0:1, 0:1], min_val=0, max_val=MAX_OVER)
            with act.Fori(0, NEXP // RING) as i:
                for b in range(RING):
                    expert(RING * i + b, b % 2, RING * i + b,
                           lambda b=b: act.wait_ge(rows_scattered[b % 2], (1 + 2 * i + b // 2) * 16))
            for b in range(2):
                act.wait_ge(rows_scattered[b], SCATTERED)
            with act.If(n_over > 0):
                with act.Fori(0, MAX_OVER) as j:
                    with act.If(j < n_over):
                        expert(NEXP + j, 0, NEXP + j, lambda: act.wait_ge(rows_scattered[0], SCATTERED + j * 16))

            for t in range(T):
                act.wait_ge(x3_ready, t + 1)
                if t:
                    act.wait_ge(x3_squared, t)
                act.activation(junk3, x_sb[:, t, :], ACT.Square, accum_out=ss3[:, t:t + 1]).then_inc(x3_squared, 1)
            root(rr3, ss3, x3_squared, T)
            act.wait_ge(x3_rstd, 1)
            for t in range(T):
                for half in range(2):
                    act.wait_ge(pg_mm, 2 * t + half + 1)
                    if t >= 2:
                        act.wait_ge(x4_squared, t - 1)
                    act.activation(sg6[:, t % 2, half * 512:(half + 1) * 512],
                                   (PA, PB, S_1, S_4)[(2 * t + half) % 4][:, :],
                                   ACT.Sigmoid, scale=rr3[:, t:t + 1]).then_inc(pg_sig, 1)
                act.wait_ge(x4_ready, t + 1)
                act.activation(sg6[:, t % 2], x_sb[:, t, :], ACT.Square, accum_out=ss4[:, t:t + 1]).then_inc(x4_squared, 1)
                root(rr4[:, t:t + 1], ss4[:, t:t + 1], x4_squared, t + 1)

        @block.tensor
        def _(pe):
            def mm(out, lhsT, rhs, start=True, stop=True):
                return pe.matmul(out, lhsT, rhs, start=start, stop=stop)

            def split_product(out, high, low, rhs_high, rhs_low, first, last_one):
                mm(out, high, rhs_high, first, False)
                mm(out, high, rhs_low, False, False)
                return mm(out, low, rhs_high, False, last_one)

            pe.sem_inc(cm_done, CM_CREDIT)
            for guard in (*bank_read, att_out, pt_ready, y_ready, sgo_ready, merged, y_low, y_high):
                pe.sem_inc(guard, FREE)
            pe.wait_ge(ident_loaded, 16)

            def gates(t):
                pe.wait_ge(h_ready, 2 * (t + 1))
                for k in range(KD):
                    last = mm(MM[:, t * 8:t * 8 + 8], hT[:, k, t * P:(t + 1) * P], wtm[:, 0, k * 8:k * 8 + 8],
                              k == 0, k == KD - 1)
                last.then_inc(if_projected, 1)

            pe.wait_ge(w_if_loaded, 16)
            for t in range(T):
                pe.wait_ge(x_normed, t + 1)
                for half in range(2):
                    if t:
                        pe.wait_ge(h_ready, 2 * t + half - 1)
                    for k in range(4):
                        last = pe.transpose((PA, PB)[half][:, k * P:(k + 1) * P],
                                            mT_tok[:, t, (4 * half + k) * P:(4 * half + k + 1) * P], ident)
                    last.then_inc(x_turned, 1)
                if t:
                    gates(t - 1)
            gates(T - 1)
            pe.wait_ge(consts_loaded, 16)

            def turn_gates():
                pe.wait_ge(if_ready, 1)
                for t in range(T):
                    pe.transpose(S_1[0:4, t * P:(t + 1) * P], ifs[:, t, 0:4], ident)
                pe.wait_ge(lf_ready, 1)
                for t in range(T):
                    last = pe.transpose(S_4[0:4, t * P:(t + 1) * P], lft[:, 0, t, :], ident)
                last.then_inc(if_turned, 1)

            def spread_gates():
                pe.wait_ge(prefix_ready, 4)
                for h in range(4):
                    last = mm((S_1, S_4, S_16, OUT)[h][:, :], const("sel", 4)[:, h * P:(h + 1) * P], rows[0:4, 2, :])
                last.then_inc(max_spread, 1)
                pe.wait_ge(em_ready, 1)
                for q, row in enumerate((1, 4)):
                    for t in range(T):
                        last = pe.transpose(TR[:, (q * T + t) * 4:(q * T + t) * 4 + 4],
                                            rows[0:4, row, t * P:(t + 1) * P], ident[0:4, 0:4])
                last.then_inc(cols_turned, 1)

            def one_round(r, first=False):
                def unit(u):
                    return r * 8 + u + 1

                for n in range(CM_ORDER):
                    pe.wait_ge(cm_split, r * CM_ORDER + n + 1)
                    pe.wait_ge(bank_read[n % 2], FREE + 6 * r + n // 2)
                    for k in range(KD):
                        if first and n == 0:
                            pe.wait_ge(h_split[k >= H_DVE], k + 1 - H_DVE * (k >= H_DVE))
                        part = slice(k * P, (k + 1) * P)
                        last = split_product((PA, PB)[n % 2][:, :], cm_high[n % 2][:, part], wcm_low[:, n % 4, part],
                                             h_high[:, k, :], h_low[:, k, :], k == 0, k == KD - 1)
                    last.then_inc(cm_done, 1)
                    if first and n < 2:
                        (turn_gates, spread_gates)[n]()

                def scores(u):
                    s, i = divmod(u, 4)
                    if u:
                        pe.wait_ge(negmax_ready, unit(u - 1))
                    lo, hi = s * HEAD, (s + 1) * HEAD
                    for g, bank in enumerate((S_1, S_4, S_16)):
                        k0 = max(0, i - 1) * P if g == 0 else 0
                        n = (i + 1) * P - k0
                        last = mm(bank[:, 0:n], qT[lo:hi, g, i * P:(i + 1) * P], kT[lo:hi, k0:k0 + n])
                    last.then_inc(scores_done, 1)

                def turn(u):
                    pe.wait_ge(probs_ready, unit(u))
                    pe.wait_ge(pt_ready, FREE + r * 8 + u)
                    for j in range(u % 4 + 1):
                        last = pe.transpose(TR[:, j * P:(j + 1) * P], psm[:, u % 2, j * P:(j + 1) * P], ident)
                    last.then_inc(probs_turned, 1)

                def pv(u):
                    s, i = divmod(u, 4)
                    pe.wait_ge(pt_ready, FREE + unit(u))
                    if i == 0:
                        pe.wait_ge(att_out, FREE + 2 * r + s)
                    for j in range(i + 1):
                        last = mm(OUT[:, i * HEAD:(i + 1) * HEAD], pT_sb[:, u % 2, j * P:(j + 1) * P],
                                  tmv[:, j, s * HEAD:(s + 1) * HEAD], j == 0, j == i)
                    last.then_inc(pv_done, 1)

                for u in range(8):
                    if u == 0:
                        if first:
                            pe.wait_ge(mb_ready, 5)
                        pe.wait_ge(bank_read[0], FREE + 6 * r + 4)
                        pe.wait_ge(bank_read[1], FREE + 6 * r + 4)
                    scores(u)
                    if u < T:
                        if u == 0:
                            pe.wait_ge(tm_split, r + 1)
                        pe.wait_ge(bank_read[u % 2], FREE + 6 * r + 4 + u // 2)
                        for k in range(KD):
                            part = slice(u * P, (u + 1) * P)
                            last = split_product((PA, PB)[u % 2][:, 0:3 * P], h_high[:, k, part], h_low[:, k, part],
                                                 wtm_high[:, k, :], wtm_low[:, k, :], k == 0, k == KD - 1)
                        last.then_inc(tm_done, 1)
                    else:
                        j = u - T
                        if j == 0:
                            pe.wait_ge(qk_ready, 2 * (r + 1))
                            pe.wait_ge(y_ready, FREE + 2 * r)
                        else:
                            pe.wait_ge(m_weighted, r * T + j)
                        mm(MM[:, 0:(T - j) * P], qk[:, 1, j * P:(j + 1) * P], qk[:, 0, j * P:]).then_inc(m_scores, 1)
                    if u >= 2:
                        pv(u - 2)
                    if u >= 1:
                        turn(u - 1)
                pe.wait_ge(negmax_ready, unit(7))
                pe.wait_ge(m_weighted, (r + 1) * T)
                for i in range(T):
                    bank, at = (S_1, S_4)[i // 2], (i % 2) * (DH + 1)
                    for j in range(i + 1):
                        q0 = M_AT[j] + (i - j) * P
                        last = mm(bank[:, at:at + DH + 1], wms[:, q0:q0 + P], tmv[:, j, 2 * P:3 * P + 1], j == 0, j == i)
                last.then_inc(m_num, 1)
                pv(6)
                turn(7)
                pv(7)
                pe.wait_ge(ym_ready, r + 1)
                for i in range(T):
                    last = pe.transpose(MM[:, i * P:(i + 1) * P], ym[:, i, :], ident)
                last.then_inc(ym_turned, 1)
                pe.wait_ge(att_out, FREE + 2 * r + 2)
                for i in range(T):
                    last = pe.transpose(TR[:, i * P:(i + 1) * P], oatt[:, i, :], ident)
                last.then_inc(att_turned, 1)
                pe.wait_ge(y_ready, FREE + 2 * r + 1)

            one_round(0, first=True)
            with pe.Fori(1, ROUNDS) as r:
                one_round(r)

            pe.wait_ge(conv_ready, ROUNDS)
            for c in range(ROUNDS):
                last = mm(TR[:, :], const("mean"), yT[:, 2, c, :], c == 0, c == ROUNDS - 1)
            last.then_inc(ln_mm, 1)
            for b in range(2):
                pe.wait_ge(bank_read[b], FREE + 6 * ROUNDS)

            def merge_tile(h, s, first=False):
                dt = 2 * h + s
                pe.wait_ge(mw_loaded[s], (h + 1) * 32)
                for br in range(3):
                    pe.wait_ge(gate_split, 3 * dt + br + 1)
                    pe.wait_ge(gate_read, 3 * dt + br + 1)
                    for k in range(KD):
                        part = slice(k * P, (k + 1) * P)
                        last = split_product((PA, S_1, S_16)[br][:, :], gate_high[br][:, part], wg_low[s][:, br, part],
                                             h_high[:, k, :], h_low[:, k, :], k == 0, k == KD - 1)
                    last.then_inc(gate_done, 1)
                    if first and br == 0:
                        pe.wait_ge(ln_act, ROUNDS)
                        pe.wait_ge(y_ready, FREE + 2 * ROUNDS)
                        for c in range(ROUNDS):
                            last = mm(MM[:, :], const("mean"), lnt[:, c, :], c == 0, c == ROUNDS - 1)
                        last.then_inc(ln_mm, 1)
                    if first and br == 2:
                        pe.wait_ge(yconv_ready, ROUNDS)
                    pe.wait_ge(branch_read, 3 * dt + br + 1)
                    for k in range(4):
                        last = mm((PB, S_4, OUT)[br][:, :], wb[s][:, br, k * P:(k + 1) * P], yT[:, br, k, :],
                                  k == 0, k == 3)
                    last.then_inc(branch_done, 1)

            merge_tile(0, 0, first=True)
            merge_tile(0, 1)
            with pe.Fori(1, KD // 2) as h:
                for s in range(2):
                    merge_tile(h, s)

            def project(t):
                for half in range(2):
                    n = 2 * t + half
                    if n >= 4:
                        pe.wait_ge(x2_ready, n - 3)
                    for k in range(KD):
                        last = mm((PA, PB, S_1, S_4)[n % 4][:, :], merged_T[:, k, t * P:(t + 1) * P],
                                  wo[:, k, half * 512:(half + 1) * 512], k == 0, k == KD - 1)
                    last.then_inc(x2_mm, 1)

            def turn_rows(t, rows_ready, value, done, read):
                pe.wait_ge(rows_ready, value)
                for half in range(2):
                    if t:
                        pe.wait_ge(read, 2 * t + half - 1)
                    for k in range(4):
                        last = pe.transpose((S_16, OUT)[half][:, k * P:(k + 1) * P],
                                            x_sb[:, t, (4 * half + k) * P:(4 * half + k + 1) * P], ident)
                    last.then_inc(done, 1)

            pe.wait_ge(wo_loaded, 16)
            pe.wait_ge(merged, FREE + KD)
            for t in range(T):
                project(t)
                if t:
                    turn_rows(t - 1, x2_ready, 2 * t, x2_turned, h2_ready)
            turn_rows(T - 1, x2_ready, 2 * T, x2_turned, h2_ready)
            pe.wait_ge(h2_ready, 2 * T)
            for t in range(T):
                for k in range(KD):
                    last = mm(MM[:, t * 36:(t + 1) * 36], hT[:, k, t * P:(t + 1) * P], wr_sb[:, k, :],
                              k == 0, k == KD - 1)
            last.then_inc(logits_done, 1)

            def ple(t):
                for half in range(2):
                    n = 2 * t + half
                    if n >= 4:
                        pe.wait_ge(ple_copied, n - 3)
                    for k in range(2):
                        last = mm((PA, PB, S_1, S_4)[n % 4][:, :], p_in[:, k, t * P:(t + 1) * P],
                                  pple_w[:, k, half * 512:(half + 1) * 512], k == 0, k == 1)
                    last.then_inc(ple_mm, 1)

            pe.wait_ge(onehots, 1)
            for t in range(T + 1):
                for q in range(min(t + 1, T)):
                    last = mm(TR[:, t * NEXP:(t + 1) * NEXP], const("upper") if q == t else ones, tmp[:, q, :],
                              q == 0, q == min(t, T - 1))
            last.then_inc(counts_done, 1)
            pe.wait_ge(pw_loaded, 32)
            pe.wait_ge(x2_ready, 2 * T)
            pe.wait_ge(n2_stored, T * 16)
            for t in range(T):
                ple(t)

            def turn_block(n, b2, gathered, value, first=False):
                pe.wait_ge(gathered, value)
                if not first:
                    pe.wait_ge(xT_ready, n)
                for k in range(KD):
                    last = (pe.matmul if k == 0 else pe.transpose)(
                        TR[:, k * BLK:(k + 1) * BLK], xr[b2][:, k * P:(k + 1) * P], ident[0:BLK, 0:BLK],
                        **(dict(start=True, stop=True) if k == 0 else {}))
                last.then_inc(rows_turned, 1)

            def up(n, b2, w):
                for m in range(4):
                    for k in range(KD):
                        last = mm((MM, S_1)[m // 2][:, m % 2 * BLK:(m % 2 + 1) * BLK],
                                  w[:, k * 512 + m * P:k * 512 + (m + 1) * P],
                                  xT[b2][:, k, :], k == 0, k == KD - 1)
                    if m % 2:
                        last.then_inc((g_done, u_done)[m // 2], 1)

            def down(n, w):
                pe.wait_ge(hx_ready, n + 1)
                pe.wait_ge(y_low, FREE + n)
                pe.wait_ge(y_high, FREE + n)
                for half in range(2):
                    for j in range(2):
                        at = 4096 + j * 1024 + half * 512
                        last = mm((OUT, S_16)[half][0:BLK, :], hx[:, j, :], w[:, at:at + 512], j == 0, j == 1)
                    last.then_inc(down_done, 1)

            pe.wait_ge(ple_copied, 2 * T)
            pe.wait_ge(table_loaded, 16)
            turn_block(0, 0, rows_gathered[0], 16, first=True)
            pe.wait_ge(routed, 2)
            n_over = pe.value_load(ctl[0:1, 0:1], min_val=0, max_val=MAX_OVER)
            with pe.Fori(0, NEXP // RING) as i:
                for b in range(RING):
                    n = RING * i + b
                    pe.wait_ge(we_loaded[b], (i + 1) * 16)
                    pe.wait_ge(xT_ready, n + 1)
                    up(n, b % 2, we[b])
                    turn_block(n + 1, (b + 1) % 2, rows_gathered[(b + 1) % 2], (2 * i + (b + 1) // 2 + 1) * 16)
                    down(n, we[b])
            with pe.If(n_over > 0):
                with pe.Fori(0, MAX_OVER) as j:
                    with pe.If(j < n_over):
                        turn_block(NEXP + 1 + j, 0, ov_gathered, (j + 1) * 16)
                        pe.wait_ge(ov_w, (j + 1) * 16)
                        pe.wait_ge(xT_ready, NEXP + 2 + j)
                        up(NEXP + j, 1, we[3])
                        down(NEXP + j, we[3])

            pe.wait_ge(y_low, FREE + NEXP)
            pe.wait_ge(pg_loaded, 48)
            turn_rows(0, x3_ready, 1, x3_turned, h3_ready)
            for t in range(T):
                pe.wait_ge(h3_ready, 2 * (t + 1))
                for half in range(2):
                    n = 2 * t + half
                    if n >= 4:
                        pe.wait_ge(pg_sig, n - 3)
                    for k in range(KD):
                        last = mm((PA, PB, S_1, S_4)[n % 4][:, :], hT[:, k, t * P:(t + 1) * P],
                                  we[k // 4][:, (k % 4) * D + half * 512:(k % 4) * D + (half + 1) * 512],
                                  k == 0, k == KD - 1)
                    last.then_inc(pg_mm, 1)
                    if half == 0 and t + 1 < T:
                        turn_rows(t + 1, x3_ready, t + 2, x3_turned, h3_ready)

        @block.vector
        def _(dve):
            steps = [0]

            def chain(ins):
                steps[0] += 1
                ins.then_inc(dve_step, 1)
                dve.wait_ge(dve_step, steps[0])

            dve.memset(small[:, 94:95], 1.0).then_inc(cell_set, 1)
            dve.memset(ypad[:, 0:CONV_K - 1], 0.0)
            dve.memset(raw[:, :, 0:MCONV_K - 1], 0.0)
            dve.memset(tmv[:, :, 3 * P:3 * P + 1], 1.0)
            chain(dve.memset(rows[0:4, 0, :], 1.0))
            dve.wait_ge(chan_loaded, 16)

            def h_out(t, banks2, turned, gain, ready_sem):
                for half in range(2):
                    dve.wait_ge(turned, 2 * t + half + 1)
                    dve.tensor_tensor(hT[:, 4 * half:4 * half + 4, t * P:(t + 1) * P],
                                      banks2[half][:, :].rearrange("p (k s) -> p k s", k=4),
                                      chn[:, gain + 4 * half:gain + 4 * half + 4].unsqueeze(2).to_broadcast([P, 4, P]),
                                      ALU.mult).then_inc(ready_sem, 1)

            rooted_seen = [0]

            def rstd(root, total, done=None):
                rooted_seen[0] += 1
                dve.wait_ge(rooted, rooted_seen[0])
                chain(dve.tensor_scalar(total, total, 1.0 / D, EPS, ALU.mult, ALU.add))
                chain(dve.reciprocal(root, root))
                chain(dve.tensor_tensor(total, total, root, ALU.mult))
                chain(dve.tensor_tensor(total, total, root, ALU.mult))
                chain(dve.tensor_scalar(total, total, -0.5, 1.5, ALU.mult, ALU.add))
                last = dve.tensor_tensor(root, root, total, ALU.mult)
                if done:
                    last.then_inc(done[0], 1)
                    dve.wait_ge(*done)
                else:
                    chain(last)

            for t in range(T):
                rstd(rr[:, t:t + 1], ss[:, t:t + 1])
                dve.tensor_scalar(mT_tok[:, t, :], x_sb[:, t, :], rr[:, t:t + 1], None, ALU.mult).then_inc(x_normed, 1)
                if t:
                    h_out(t - 1, (PA, PB), x_turned, G_MIX, h_ready)
            h_out(T - 1, (PA, PB), x_turned, G_MIX, h_ready)

            dve.wait_ge(h_ready, 2 * T)
            for k in range(KD):
                dve.tensor_copy(h_high[:, k, :], hT[:, k, :]).then_inc(h_rounded, 1)
            dve.wait_ge(if_projected, T)
            dve.wait_ge(h_rounded, H_DVE)
            for k in range(H_DVE):
                dve.tensor_tensor(h_low[:, k, :], hT[:, k, :], h_high[:, k, :].bitcast(F32),
                                  ALU.subtract).then_inc(h_split[0], 1)
            def low_part(high, low, weights, rounded_before, done):
                dve.wait_ge(rounded, rounded_before + 1)
                dve.tensor_tensor(low, weights, high.bitcast(F32), ALU.subtract).then_inc(done, 1)

            def cm_tile(r, n):
                low_part(cm_high[n % 2], wcm_low[:, n % 4, :], wcm[:, n % 4, :],
                         r * (CM_ORDER + 1) + n + (n > TM_AFTER), cm_split)

            def gate_tile(h, s, br):
                low_part(gate_high[br], wg_low[s][:, br, :], wg[s][:, br, :],
                         ROUNDS * (CM_ORDER + 1) + 3 * (2 * h + s) + br, gate_split)

            for n in range(2):
                cm_tile(0, n)
            dve.wait_ge(params_loaded, N_PARAMS * 16)
            dve.wait_ge(consts_loaded, 16)
            dve.wait_ge(if_projected, T)
            dve.tensor_tensor(ifs[:, :, :], MM[:, 0:32].rearrange("p (t c) -> p t c", t=T),
                              if_b[:, :].unsqueeze(1).to_broadcast([P, T, 8]), ALU.add).then_inc(if_ready, 1)
            dve.wait_ge(if_ready, 1)
            dve.wait_ge(act_step, 3)
            dve.scalar_tensor_tensor(lft[:, 0], ifs[:, :, 4:8], 0.0, lft[:, 2], ALU.min, ALU.subtract).then_inc(lf_ready, 1)
            dve.wait_ge(if_turned, 1)
            dve.tensor_tensor_scan(rows[0:4, 3, :], rows[0:4, 0, :], S_4[0:4, :], 0.0, ALU.mult, ALU.add).then_inc(prefix_ready, 1)
            dve.wait_ge(prefix_ready, 1)
            dve.tensor_tensor(rows[0:4, 1, :], S_1[0:4, :], rows[0:4, 3, :], ALU.subtract).then_inc(prefix_ready, 1)
            dve.wait_ge(prefix_ready, 2)
            dve.tensor_tensor_scan(rows[0:4, 2, :], rows[0:4, 1, :], rows[0:4, 1, :], 0.0, ALU.max, ALU.max).then_inc(prefix_ready, 2)
            dve.wait_ge(prefix_ready, 4)
            dve.tensor_tensor(rows[0:4, 3, :], rows[0:4, 3, :], rows[0:4, 2, :], ALU.add).then_inc(prefix_ready, 1)
            dve.wait_ge(max_spread, 1)
            for h in range(4):
                dve.tensor_copy(mb[:, h, :], (S_1, S_4, S_16, OUT)[h][:, :]).then_inc(mb_ready, 1)
            dve.wait_ge(cols_turned, 1)
            dve.tensor_copy(ucol[:, :, :], TR[:, 0:16].rearrange("p (t h) -> p t h", t=T))
            dve.tensor_copy(ecol[:, :, :], TR[:, 16:32].rearrange("p (t h) -> p t h", t=T)).then_inc(mb_ready, 1)
            dve.sem_inc(branch_read, 3)

            def one_round(r, last=False):
                def unit(u):
                    return r * 8 + u + 1

                def conv(value):
                    dve.wait_ge(conv_step, r * CONV_STEPS + value)

                w31 = lambda j: chn[:, bass.ds(CONV_W + r * CONV_K + j, 1)]
                wq = lambda j: chn[:, bass.ds(MCONV + r * 10 + j, 1)]
                cm_tile(r, 2)
                cm_tile(r, 3)
                dve.wait_ge(bank_read[0], FREE + 6 * r + 1)
                dve.wait_ge(cm_done, CM_CREDIT + r * CM_ORDER + 2)
                dve.tensor_tensor(ypad[:, CONV_K - 1:], PB[:, :], sgt, ALU.mult).then_inc(bank_read[1], 1)
                dve.wait_ge(bank_read[1], FREE + 6 * r + 1)
                dve.tensor_scalar(cacc[:, 0], ypad[:, 0:SEQ], w31(0), chn[:, bass.ds(CONV_B + r, 1)],
                                  ALU.mult, ALU.add).then_inc(conv_step, 1)
                dve.tensor_scalar(cacc[:, 1], ypad[:, 1:1 + SEQ], w31(1), None, ALU.mult).then_inc(conv_step, 1)
                for j in range(2, CONV_K):
                    if j in CM_TILES_AT:
                        cm_tile(r, CM_TILES_AT[j])
                    if j == TM_TILE_AT:
                        dve.wait_ge(tm_loaded, (r + 1) * 16)
                        low_part(wtm_high, wtm_low, wtm, r * (CM_ORDER + 1) + TM_AFTER + 1, tm_split)
                    conv(j - 1)
                    dve.scalar_tensor_tensor(cacc[:, j % 2], ypad[:, j:j + SEQ], w31(j), cacc[:, j % 2],
                                             ALU.mult, ALU.add).then_inc(conv_step, 1)
                conv(CONV_K)
                dve.tensor_tensor(yT[:, 2, bass.ds(r, 1), :], cacc[:, 0], cacc[:, 1], ALU.add).then_inc(conv_ready, 1)
                dve.wait_ge(bank_read[0], FREE + 6 * r + 2)
                dve.wait_ge(bank_read[1], FREE + 6 * r + 2)
                for c in range(2):
                    dve.tensor_scalar(qk[:, c], raw[:, c, 0:SEQ], wq(4 * c), wq(8 + c), ALU.mult, ALU.add)\
                       .then_inc(conv_step, 1)
                    for j in range(1, MCONV_K):
                        conv(CONV_K + 4 * c + j)
                        dve.scalar_tensor_tensor(qk[:, c], raw[:, c, j:j + SEQ], wq(4 * c + j), qk[:, c],
                                                 ALU.mult, ALU.add).then_inc(conv_step, 1)
                for c in range(2):
                    dve.wait_ge(mq_sig, 2 * r + c + 1)
                    dve.scalar_tensor_tensor(qk[:, c], qk[:, c], 1.0 if c == 0 else DH ** -0.5, sqk[:, c],
                                             ALU.mult, ALU.mult).then_inc(qk_ready, 1)

                def out_of_slot(s):
                    dve.wait_ge(exps_done, unit(4 * s + 3))
                    dve.reciprocal(rden[:, 4 * s:4 * s + 4], den[:, 4 * s:4 * s + 4]).then_inc(rden_ready, 1)
                    dve.wait_ge(rden_ready, 2 * r + s + 1)
                    dve.wait_ge(pv_done, unit(4 * s + 3))
                    dve.tensor_tensor(oatt[:, :, s * HEAD:(s + 1) * HEAD],
                                      OUT[:, 0:T * HEAD].rearrange("p (i c) -> p i c", i=T),
                                      rden[:, 4 * s:4 * s + 4].unsqueeze(2).to_broadcast([P, T, HEAD]),
                                      ALU.mult).then_inc(att_out, 1)

                for u in range(8):
                    s, i = divmod(u, 4)
                    n, near = (i + 1) * P, min(i + 1, 2) * P
                    if u % 4 == 0:
                        dve.wait_ge(bias_ready, 6 * r + 3 * (s + 1))
                    if u >= 2:
                        dve.wait_ge(probs_ready, unit(u - 2))
                    dve.wait_ge(scores_done, unit(u))
                    dve.memset(takes_wait[:, 2:3], 0.0)
                    for g, (bank, at, width, b0) in enumerate(((S_4, 0, n, 512 - n), (S_16, n, n, 1024 - n),
                                                               (S_1, 2 * n, near, 1280 - near))):
                        dve.tensor_tensor_reduce(out=sc[:, u % 2, at:at + width], in0=bank[:, 0:width],
                                                 in1=bias[:, s, b0:b0 + width], scale=1.0, scalar=-3e38,
                                                 op0=ALU.add, op1=ALU.max,
                                                 accum_out=mx3[:, u % 2, g:g + 1]).then_inc(biased, 1)
                    dve.wait_ge(biased, 3 * unit(u))
                    dve.tensor_reduce(nmx[:, u % 2:u % 2 + 1], mx3[:, u % 2, :], AXX, ALU.max, negate=True)\
                       .then_inc(negmax_ready, 1)
                    if u >= T:
                        j = u - T
                        dve.wait_ge(m_scores, r * T + j + 1)
                        dve.wait_ge(m_weights, 7 * r + min(2 * (j + 1), 7))
                        at, width = M_AT[j], (T - j) * P
                        dve.tensor_tensor(wms[:, at:at + width], MM[:, 0:width], wm[:, at:at + width], ALU.mult)\
                           .then_inc(m_weighted, 1)
                    if u >= 4 and not last and u < 6:
                        cm_tile(r + 1, u - 4)
                    if last and u >= 4 and u < 7:
                        gate_tile(0, 0, u - 4)
                    if u == 6:
                        out_of_slot(0)
                dve.wait_ge(m_num, r + 1)
                for q, bank in enumerate((S_1, S_4)):
                    dve.tensor_copy(md[:, 0, 2 * q:2 * q + 2].unsqueeze(2),
                                    bank[:, 0:2 * (DH + 1)].rearrange("p (i c) -> p i c", i=2)[:, :, DH:DH + 1])\
                       .then_inc(md_step, 1)
                dve.wait_ge(md_step, 5 * r + 2)
                dve.scalar_tensor_tensor(md[:, 1, :], md[:, 0, :], -1.0, md[:, 0, :], ALU.mult, ALU.max).then_inc(md_step, 1)
                dve.wait_ge(md_step, 5 * r + 3)
                dve.tensor_tensor(md[:, 1, :].unsqueeze(2), md[:, 1, :].unsqueeze(2), ecol[:, :, bass.ds(r, 1)], ALU.max)\
                   .then_inc(md_step, 1)
                dve.wait_ge(md_step, 5 * r + 4)
                dve.reciprocal(md[:, 1, :], md[:, 1, :]).then_inc(md_step, 1)
                dve.wait_ge(md_step, 5 * r + 5)
                dve.wait_ge(sgo_ready, FREE + r + 1)
                for i in range(T):
                    at = (i % 2) * (DH + 1)
                    last = dve.scalar_tensor_tensor(ym[:, i, :], (S_1, S_4)[i // 2][:, at:at + DH], md[:, 1, i:i + 1],
                                                    sgo[:, i, :], ALU.mult, ALU.mult)
                last.then_inc(ym_ready, 1)
                out_of_slot(1)

            with dve.Fori(0, ROUNDS - 1) as r:
                one_round(r)
            one_round(ROUNDS - 1, last=True)

            dve.wait_ge(ln_mm, 1)
            for c in range(ROUNDS):
                dve.tensor_tensor(yT[:, 2, c, :], yT[:, 2, c, :], TR[:, :], ALU.subtract).then_inc(ln_step, 1)
            dve.wait_ge(ln_mm, 2)
            dve.tensor_scalar(rst, MM[:, :], EPS, None, ALU.add).then_inc(ln_step, 1)
            dve.wait_ge(ln_root, 1)
            chain(dve.reciprocal(lnr, lnr))
            chain(dve.tensor_tensor(rst, rst, lnr, ALU.mult))
            chain(dve.tensor_tensor(rst, rst, lnr, ALU.mult))
            chain(dve.tensor_scalar(rst, rst, -0.5, 1.5, ALU.mult, ALU.add))
            chain(dve.tensor_tensor(rst, rst, lnr, ALU.mult))
            for c in range(ROUNDS):
                dve.tensor_tensor(yT[:, 2, c, :], yT[:, 2, c, :], rst, ALU.mult).then_inc(ln_step, 1)
            for c in range(ROUNDS):
                dve.wait_ge(ln_step, 6 + c)
                dve.wait_ge(ln_act, 2 * ROUNDS - 3 + c)
                chain(dve.tensor_scalar(yT[:, 2, c, :], yT[:, 2, c, :], chn[:, LN_G + c:LN_G + c + 1],
                                        chn[:, LN_B + c:LN_B + c + 1], ALU.mult, ALU.add))
                dve.tensor_tensor(yT[:, 2, c, :], yT[:, 2, c, :], sgl[:, c], ALU.mult).then_inc(yconv_ready, 1)

            def merge(h, s, last=False):
                dt = 2 * h + s
                for br in range(3):
                    dve.wait_ge(gate_read, 3 * dt + br + 4)
                    if not last:
                        gate_tile(h + s, 1 - s, br)
                    dve.wait_ge(branch_done, 3 * dt + br + 1)
                    dve.tensor_tensor(mp[:, br], (PB, S_4, OUT)[br][:, :], sgm[:, br], ALU.mult).then_inc(branch_read, 1)
                    if br == 1:
                        dve.wait_ge(branch_read, 3 * dt + 5)
                        dve.tensor_tensor(mp[:, 0], mp[:, 0], mp[:, 1], ALU.add).then_inc(merge_step, 1)
                dve.wait_ge(branch_read, 3 * dt + 6)
                dve.wait_ge(merge_step, dt + 1)
                dve.tensor_tensor(merged_T[:, dt:dt + 1, :] if last else merged_T[:, bass.ds(dt, 1), :],
                                  mp[:, 0:1], mp[:, 2:3], ALU.add).then_inc(merged, 1)

            with dve.Fori(0, KD // 2 - 1) as h:
                for s in range(2):
                    merge(h, s)
            merge(KD // 2 - 1, 0)
            merge(KD // 2 - 1, 1, last=True)

            for t in range(T):
                for half in range(2):
                    dve.wait_ge(x2_mm, 2 * t + half + 1)
                    if half == 0:
                        dve.wait_ge(x_loaded[t], 32)
                    part = x_sb[:, t, half * 512:(half + 1) * 512]
                    dve.tensor_tensor(part, part, (PA, PB, S_1, S_4)[(2 * t + half) % 4][:, :], ALU.add).then_inc(x2_ready, 1)
                if t:
                    h_out(t - 1, (S_16, OUT), x2_turned, G_FFN, h2_ready)
                if t == T - 1:
                    h_out(t, (S_16, OUT), x2_turned, G_FFN, h2_ready)
                rstd(rr2[:, t:t + 1], ss2[:, t:t + 1])
                dve.tensor_scalar(n2[:, t, :], x_sb[:, t, :], rr2[:, t:t + 1], None, ALU.mult).then_inc(n2_ready, 1)

            def spread(ap, shape, axis):
                return ap.unsqueeze(axis).to_broadcast(shape)

            def first_max(onehot, value, rev, scratch, top, n):
                chain(dve.tensor_reduce(top, value, AXX, ALU.max))
                chain(dve.tensor_tensor(scratch, value, spread(top, [P, T, n], 2), ALU.is_equal))
                chain(dve.tensor_tensor(scratch, scratch, spread(rev, [P, T, n], 1), ALU.mult))
                chain(dve.tensor_reduce(per[:, 11, 0, :], scratch, AXX, ALU.max))
                chain(dve.tensor_tensor(onehot, scratch, spread(per[:, 11, 0, :], [P, T, n], 2), ALU.is_equal))

            dve.wait_ge(logits_done, 1)
            for t in range(T):
                last = dve.scalar_tensor_tensor(rl[:, t, :], MM[:, t * 36:(t + 1) * 36], rr2[:, t:t + 1], r_b[:, :],
                                                ALU.mult, ALU.add)
            chain(last)
            top_g, p_g, top_1, top_2 = (per[:, q, 0, :] for q in (1, 2, 3, 4))
            first_max(oh4[:, :, :], rl[:, :, 0:NGROUP], const("rev4"), t4[:, :, :], top_g, NGROUP)
            dve.tensor_tensor(t4[:, :, :], rl[:, :, 0:NGROUP], spread(top_g, [P, T, NGROUP], 2), ALU.subtract)\
               .then_inc(shifted, 1)
            chain(dve.tensor_scalar(oh4[:, :, :], oh4[:, :, :], 1.0, BIG, ALU.subtract, ALU.mult))
            chain(dve.tensor_tensor(le[:, :, :].rearrange("p t (g e) -> p t g e", g=NGROUP),
                                    rl[:, :, NGROUP:].rearrange("p t (g e) -> p t g e", g=NGROUP),
                                    spread(oh4[:, :, :], [P, T, NGROUP, PER_GROUP], 3), ALU.add))
            first_max(oh[:, 0], le[:, :, :], const("rev32"), tmp[:, 0:T, :], top_1, NEXP)
            chain(dve.scalar_tensor_tensor(le[:, :, :], oh[:, 0], -2 * BIG, le[:, :, :], ALU.mult, ALU.add))
            first_max(oh[:, 1], le[:, :, :], const("rev32"), tmp[:, 0:T, :], top_2, NEXP)
            dve.tensor_tensor(tmp[:, 0:T, :], oh[:, 0], oh[:, 1], ALU.add).then_inc(onehots, 1)
            dve.tensor_tensor(per[:, 0, 1, :], top_2, top_1, ALU.subtract).then_inc(diff_ready, 1)
            dve.wait_ge(group_exp, 1)
            chain(dve.tensor_reduce(p_g, t4[:, :, :], AXX, ALU.add))
            chain(dve.reciprocal(p_g, p_g))
            dve.wait_ge(pair_exp, 1)
            chain(dve.tensor_scalar(per[:, 5, 0, :], per[:, 0, 0, :], 1.0, None, ALU.add))
            chain(dve.reciprocal(per[:, 5, 0, :], per[:, 5, 0, :]))
            chain(dve.tensor_tensor(per[:, 6, 0, :], p_g, per[:, 5, 0, :], ALU.mult))
            chain(dve.tensor_tensor(per[:, 6, 1, :], per[:, 6, 0, :], per[:, 0, 0, :], ALU.mult))
            dve.wait_ge(counts_done, 1)
            chain(dve.tensor_copy(cc[:, :, :], TR[:, 0:(T + 1) * NEXP].rearrange("p (t e) -> p t e", e=NEXP)))
            over = over_cmp[:, :, :]
            chain(dve.tensor_tensor(over, spread(cc[:, T, :], [P, NEXP, 7], 2), spread(const("limit"), [P, NEXP, 7], 1),
                                    ALU.is_gt))
            chain(dve.tensor_reduce(ov[:, 0, :], over, AXX, ALU.add))
            chain(dve.tensor_tensor_scan(ov[:, 1, :], ones[:, 0:NEXP], ov[:, 0, :], 0.0, ALU.mult, ALU.add))
            chain(dve.tensor_tensor(ov[:, 2, :], ov[:, 1, :], ov[:, 0, :], ALU.subtract))
            oh8 = oh[:, :, :, :].rearrange("p k t e -> p (k t) e")
            flat = lambda q: per[:, q, :, :].rearrange("p k t -> p (k t)")
            rank, expert_of, over_of, beyond = (flat(q) for q in (7, 8, 9, 10))
            for k in range(2):
                chain(dve.tensor_tensor(tmp[:, k * T:(k + 1) * T, :], cc[:, 0:T, :], oh[:, k], ALU.mult))
            chain(dve.tensor_reduce(rank, tmp[:, :, :], AXX, ALU.add))
            chain(dve.tensor_tensor(tmp[:, :, :], oh8, spread(const("iota32"), [P, 8, NEXP], 1), ALU.mult))
            chain(dve.tensor_reduce(expert_of, tmp[:, :, :], AXX, ALU.add))
            chain(dve.tensor_tensor(tmp[:, :, :], oh8, spread(ov[:, 2, :], [P, 8, NEXP], 1), ALU.mult))
            chain(dve.tensor_reduce(over_of, tmp[:, :, :], AXX, ALU.add))
            past = over_cmp[:, 0:8, :]
            chain(dve.tensor_tensor(past, spread(rank, [P, 8, 7], 2), spread(const("limit"), [P, 8, 7], 1), ALU.is_ge))
            chain(dve.tensor_reduce(beyond, past, AXX, ALU.add))
            chain(dve.scalar_tensor_tensor(rank, beyond, -float(BLK), rank, ALU.mult, ALU.add))
            chain(dve.tensor_tensor(over_of, over_of, beyond, ALU.add))
            chain(dve.scalar_tensor_tensor(over_of, over_of, NEXP - 1.0, expert_of, ALU.add, ALU.subtract))
            chain(dve.tensor_scalar(beyond, beyond, 1.0, None, ALU.min))
            chain(dve.tensor_tensor(over_of, over_of, beyond, ALU.mult))
            chain(dve.tensor_tensor(over_of, over_of, expert_of, ALU.add))
            chain(dve.scalar_tensor_tensor(rank, rank, float(NBLK), over_of, ALU.mult, ALU.add))
            dve.tensor_copy(where[:, :], rank)
            dve.tensor_copy(info[:, :, 0], const("token"))
            dve.tensor_copy(info[:, :, 1], const("row"))
            dve.memset(info[:, :, 3], 0)
            dve.tensor_copy(info[:, :, 2].bitcast(F32), flat(6)).then_inc(routed, 1)
            over1 = over_ids[:, :, :]
            chain(dve.tensor_tensor(over1, ov[0:1, 1, :].unsqueeze(1).to_broadcast([1, MAX_OVER, NEXP]),
                                    const("iota15", 1).unsqueeze(2).to_broadcast([1, MAX_OVER, NEXP]), ALU.is_le))
            chain(dve.tensor_reduce(ctlf[:, 1:1 + MAX_OVER], over1, AXX, ALU.add))
            chain(dve.tensor_scalar(ctlf[:, 1:1 + MAX_OVER], ctlf[:, 1:1 + MAX_OVER], NEXP - 1.0, None, ALU.min))
            chain(dve.tensor_copy(ctlf[:, 0:1], ov[0:1, 1, NEXP - 1:NEXP]))
            dve.tensor_copy(ctl[:, :], ctlf[:, :]).then_inc(routed, 1)

            def turned_block(n, b2):
                dve.wait_ge(rows_turned, n + 1)
                dve.tensor_tensor(xT[b2], TR[:, :].rearrange("p (k s) -> p k s", k=KD),
                                  chn[:, G_FFN:G_FFN + KD].unsqueeze(2).to_broadcast([P, KD, BLK]),
                                  ALU.mult).then_inc(xT_ready, 1)

            def swiglu(n):
                gate = MM[:, 0:2 * BLK].rearrange("p (j s) -> p j s", j=2)
                upp = S_1[:, 0:2 * BLK].rearrange("p (j s) -> p j s", j=2)
                dve.wait_ge(gate_sig, n + 1)
                dve.tensor_tensor(sgx, gate, sgx, ALU.mult).then_inc(gate_mul, 1)
                dve.wait_ge(gate_mul, n + 1)
                dve.wait_ge(u_done, n + 1)
                dve.tensor_tensor(hx, upp, sgx, ALU.mult).then_inc(hx_ready, 1)

            def high_half(n, b2, col, buffer_free):
                dve.wait_ge(down_done, 2 * n + 2)
                buffer_free()
                dve.tensor_scalar(yr[b2][:, 512:1024], S_16[0:BLK, :], table_w(col), None, ALU.mult).then_inc(y_high, 1)

            dve.wait_ge(table_loaded, 16)
            turned_block(0, 0)
            dve.wait_ge(routed, 2)
            n_over = dve.value_load(ctl[0:1, 0:1], min_val=0, max_val=MAX_OVER)
            with dve.Fori(0, NEXP // RING) as i:
                for b in range(RING):
                    n = RING * i + b
                    swiglu(n)
                    turned_block(n + 1, (b + 1) % 2)
                    high_half(n, b % 2, n, lambda b=b: dve.wait_ge(rows_scattered[b % 2], (1 + 2 * i + b // 2) * 16))
            for b in range(2):
                dve.wait_ge(rows_scattered[b], SCATTERED)
            with dve.If(n_over > 0):
                with dve.Fori(0, MAX_OVER) as j:
                    with dve.If(j < n_over):
                        turned_block(NEXP + 1 + j, 1)
                        swiglu(NEXP + j)
                        high_half(NEXP + j, 0, NEXP + j, lambda: dve.wait_ge(rows_scattered[0], SCATTERED + j * 16))

            for t in range(T):
                dve.wait_ge(rows_loaded[t], 32)
                chain(dve.tensor_tensor(x_sb[:, t, :], x_sb[:, t, :], yk[t][:, 0, :], ALU.add))
                dve.tensor_tensor(x_sb[:, t, :], x_sb[:, t, :], yk[t][:, 1, :], ALU.add).then_inc(x3_ready, 1)
                if t == 0:
                    h_out(0, (S_16, OUT), x3_turned, G_PLE, h3_ready)
            h_out(1, (S_16, OUT), x3_turned, G_PLE, h3_ready)
            rstd(rr3, ss3, (x3_rstd, 1))
            for t in range(T):
                if 1 <= t < T - 1:
                    h_out(t + 1, (S_16, OUT), x3_turned, G_PLE, h3_ready)
                for half in range(2):
                    cols = slice(half * 512, (half + 1) * 512)
                    dve.wait_ge(pg_sig, 2 * t + half + 1)
                    chain(dve.tensor_tensor(pple[:, t, cols], pple[:, t, cols], sg6[:, t % 2, cols], ALU.mult))
                dve.tensor_tensor(x_sb[:, t, :], x_sb[:, t, :], pple[:, t, :], ALU.add).then_inc(x4_ready, 1)
                rstd(rr4[:, t:t + 1], ss4[:, t:t + 1])
                if t == 0:
                    dve.wait_ge(pg_loaded, 48)
                dve.scalar_tensor_tensor(x_sb[:, t, :], x_sb[:, t, :], rr4[:, t:t + 1], gfin_sb, ALU.mult, ALU.mult)\
                   .then_inc(out_ready, 1)

        @block.gpsimd
        def _(pool):
            pool.memset(table[:, :, :], OUT_OF_RANGE).then_inc(ready, 1)
            pool.wait_ge(ready, 1)
            for half in range(2):
                slots = slice(half * BLK // 2, (half + 1) * BLK // 2)
                pool.dma_start(table_dram.rearrange("(j b) w -> j b w", b=NBLK)[slots], table[slots, :, :])\
                    .then_inc(rows_scattered[half], 16)
            pool.wait_ge(if_projected, T)
            for k in range(H_DVE, KD):
                pool.wait_ge(h_rounded, k + 1)
                pool.tensor_tensor(h_low[:, k, :], hT[:, k, :], h_high[:, k, :].bitcast(F32),
                                   ALU.subtract).then_inc(h_split[1], 1)
            pool.wait_ge(consts_loaded, 16)
            pool.wait_ge(mb_ready, 5)
            with pool.Fori(0, ROUNDS) as r:
                pool.wait_ge(sgo_ready, FREE + r)
                pool.tensor_copy(slope_now[:, :], cst[:, bass.ds(_C["slope"][0] + 6 * r, 6)]).then_inc(slope_ready, 1)
                pool.wait_ge(slope_ready, r + 1)
                pool.tensor_tensor(takes_wait[:, 3:4], ones[0:1, 0:1], ones[0:1, 0:1], ALU.add)
                for s in range(2):
                    for g, (name, at, n) in enumerate((("dist1", 1024, 256), ("dist4", 0, 512), ("dist16", 512, 512))):
                        pool.tensor_scalar(bias[:, s, at:at + n], const(name),
                                           slope_now[:, 3 * s + g:3 * s + g + 1], None,
                                           ALU.mult).then_inc(bias_ready, 1)
                pool.wait_ge(qk_ready, 2 * (r + 1))
                pool.tensor_tensor(mbd.rearrange("p (t s) -> p t s", t=T),
                                   mb[:, bass.ds(r, 1), :].rearrange("p a (t s) -> p (a t) s", t=T),
                                   const("causal").unsqueeze(1).to_broadcast([P, T, P]), ALU.add).then_inc(mbd_ready, 1)
                for u in range(8):
                    i = u % 4
                    n, near = (i + 1) * P, min(i + 1, 2) * P
                    dst = psm[:, u % 2, :]
                    pool.wait_ge(exps_done, r * 8 + u + 1)
                    if u >= 2:
                        pool.wait_ge(probs_turned, r * 8 + u - 1)
                    pool.tensor_tensor(dst[:, 0:n], sc[:, u % 2, 0:n], sc[:, u % 2, n:2 * n], ALU.add).then_inc(pool_step, 1)
                    pool.wait_ge(pool_step, r * 8 + u + 1)
                    pool.tensor_tensor(dst[:, n - near:n], dst[:, n - near:n], sc[:, u % 2, 2 * n:2 * n + near],
                                       ALU.add).then_inc(probs_ready, 1)

            pool.wait_ge(merged, FREE + KD)
            pool.wait_ge(x2_mm, 2 * T)
            pool.memset(mflat[0:BLK, 0:2 * D], 0.0).then_inc(ready, 1)
            for half in range(2):
                pool.wait_ge(rows_scattered[half], 16)
            pool.wait_ge(routed, 1)
            for a in range(2 * T):
                pool.indirect_dma_start(out=table_dram, out_offset=bass.IndirectOffsetOnAxis(ap=where[:, a:a + 1], axis=0),
                                        in_=info[:, a, :], in_offset=None, bounds_check=BLK * NBLK - 1,
                                        oob_is_err=False).then_inc(table_written, 16)
            pool.wait_ge(table_loaded, 16)
            pool.wait_ge(n2_stored, T * 16)
            pool.wait_ge(ready, 2)

            def take_wait(cell):
                pool.tensor_tensor(takes_wait[:, cell:cell + 1], ones[0:1, 0:1], ones[0:1, 0:1], ALU.add)

            def gather(b2, col, done, count):
                take_wait(0)
                pool.tensor_copy(gidx[:, b2:b2 + 1, :], table[:, bass.ds(col, 1), 0:2]).then_inc(idx_copied, 1)
                pool.wait_ge(idx_copied, count + 1)
                take_wait(1)
                pool.indirect_dma_start(out=xr[b2], out_offset=None, in_=normed,
                                        in_offset=bass.IndirectOffsetOnAxis(ap=gidx[:, b2, 0:1], axis=0),
                                        bounds_check=SEQ - 1, oob_is_err=False).then_inc(done, 16)

            def scatter(b2, col, done, count):
                take_wait(0)
                pool.tensor_copy(sidx[:, b2:b2 + 1, :], table[:, bass.ds(col, 1), 0:2]).then_inc(idx_copied, 1)
                pool.wait_ge(idx_copied, count + 1)
                take_wait(1)
                pool.indirect_dma_start(out=expert_rows,
                                        out_offset=bass.IndirectOffsetOnAxis(ap=sidx[:, b2, 1:2], axis=0),
                                        in_=yr[b2], in_offset=None, bounds_check=2 * SEQ - 1,
                                        oob_is_err=False).then_inc(done, 16)

            gather(0, 0, rows_gathered[0], 0)
            gather(1, 1, rows_gathered[1], 1)
            pool.wait_ge(routed, 2)
            n_over = pool.value_load(ctl[0:1, 0:1], min_val=0, max_val=MAX_OVER)
            with pool.Fori(0, NEXP // RING) as i:
                for b in range(RING):
                    n = RING * i + b
                    pool.wait_ge(rows_turned, n + 1)
                    pool.wait_ge(rows_gathered[b % 2], (2 * i + b // 2 + 1) * 16)
                    gather(b % 2, n + 2, rows_gathered[b % 2], 2 + 2 * n)
                    pool.wait_ge(y_low, FREE + n + 1)
                    pool.wait_ge(y_high, FREE + n + 1)
                    pool.wait_ge(rows_scattered[b % 2], (1 + 2 * i + b // 2) * 16)
                    scatter(b % 2, n, rows_scattered[b % 2], 3 + 2 * n)
            for b in range(2):
                pool.wait_ge(rows_gathered[b], (NEXP // 2 + 1) * 16)
                pool.wait_ge(rows_scattered[b], SCATTERED)
            pool.wait_ge(rows_turned, NEXP + 1)
            with pool.If(n_over > 0):
                with pool.Fori(0, MAX_OVER) as j:
                    with pool.If(j < n_over):
                        pool.wait_ge(rows_turned, NEXP + 1 + j)
                        gather(0, NEXP + j, ov_gathered, 2 + 2 * NEXP + 2 * j)
                        pool.wait_ge(y_low, FREE + NEXP + 1 + j)
                        pool.wait_ge(y_high, FREE + NEXP + 1 + j)
                        scatter(0, NEXP + j, rows_scattered[0], 3 + 2 * NEXP + 2 * j)
                        pool.wait_ge(rows_scattered[0], SCATTERED + (j + 1) * 16)
            pool.memset(small[:, 95:96], 0.0).then_inc(ov_all, 1)


def layout(a):
    f = lambda n: a[n][0]
    c = np.ascontiguousarray

    def tiles(w):
        return w.reshape(-1, P, w.shape[-1]).transpose(1, 0, 2)

    w = tiles(f("w_in"))
    cols = lambda at, n=P: w[:, :, at:at + n]
    cm = [[cols(at + r * P) for at in (CONV0 + CH, CONV0, MQ0, MK0, Q0, Q0 + 512, Q0 + 1024, K0)] for r in range(ROUNDS)]
    tm = [np.concatenate([cols(V0 + r * P), cols(MO0 + r * P), cols(MV0 + r * P)], -1) for r in range(ROUNDS)]
    order = ((0, "w_br_att"), (2, "w_br_mlstm"), (1, "w_br_conv"))
    gate = [[cols(GATE0 + b * D + dt * P) for b, _ in order] for dt in range(KD)]
    branch = [[tiles(f(n))[:, :, dt * P:(dt + 1) * P] for _, n in order] for dt in range(KD)]
    per = lambda v: v.reshape(-1, P).T
    mw, mb_ = f("mlstm_conv_w"), f("mlstm_conv_b")
    chan = [per(f("g_mix")), per(f("g_ffn")), per(f("g_ple"))]
    chan += [f("conv_w")[:, r * P:(r + 1) * P].T for r in range(ROUNDS)]
    chan += [per(f("conv_b")), per(f("conv_ln_g")), per(f("conv_ln_b"))]
    for r in range(ROUNDS):
        q, k = slice(r * P, (r + 1) * P), slice(CH + r * P, CH + (r + 1) * P)
        chan += [mw[:, q].T, mw[:, k].T, mb_[q][:, None], mb_[k][:, None]]
    chan += [np.full((P, 1), EPS, np.float32)]
    chan = np.concatenate(chan, 1)
    assert chan.shape == (P, NCHAN)
    experts = np.concatenate([
        np.concatenate([f("w_exp_gate"), f("w_exp_up")], -1).reshape(NEXP, KD, P, 2 * HID).transpose(0, 2, 1, 3)
        .reshape(NEXP, P, -1),
        f("w_exp_down").reshape(NEXP, 2, P, D).transpose(0, 2, 1, 3).reshape(NEXP, P, -1)], -1)
    return {k: c(v) for k, v in {
        "x": a["x"][0],
        "consts": constants(),
        "chan": chan,
        "if_bias": np.concatenate([f("mlstm_i_bias"), f("mlstm_f_bias")]),
        "r_bias": np.concatenate([f("b_router_g"), f("b_router_e")]),
        "g_final": a["g_final"],
        "w_cm": np.stack([np.stack(x) for x in cm]).reshape(ROUNDS, 8, P, KD * P),
        "w_tm": np.stack(tm),
        "w_if": cols(IF0, 8).reshape(P, -1),
        "w_gate": np.stack([np.stack(x, 1) for x in gate]).reshape(KD, P, 3, KD * P),
        "w_branch": np.stack([np.stack(x, 1) for x in branch]).reshape(KD, P, 3, 4 * P),
        "w_out": tiles(f("w_out")),
        "w_router": tiles(np.concatenate([f("w_router_g"), f("w_router_e")], -1)),
        "w_expert": experts,
        "w_pg": tiles(f("w_ple_gate")).reshape(P, 2, -1).transpose(1, 0, 2),
        "w_pp": tiles(f("w_ple_proj")),
        "pT": tiles(f("p")[0].T),
    }.items()}


def kernel(**inputs):
    import numpy as _np
    import concourse.bacc as _bacc
    from concourse import mybir as _mybir
    from concourse.bass_utils import run_bass_kernel_spmd as _run

    a = {k: _np.asarray(v) for k, v in inputs.items()}
    arrays = layout(a)
    nc = _bacc.Bacc("TRN2", target_bir_lowering=False, num_devices=1)
    args = [nc.dram_tensor(f"in_{n}", v.shape, _mybir.dt.from_np(v.dtype), kind="ExternalInput").ap()
            for n, v in arrays.items()]
    args.append(nc.dram_tensor("out_0", (SEQ, D), F32, kind="ExternalOutput").ap())
    build(nc, *args)
    r = _run(nc, [{f"in_{n}": v for n, v in arrays.items()}], core_ids=[0])
    return r.results[0]["out_0"].reshape(1, SEQ, D)
```
